# Optimizing a Trainium2 kernel written in Bass

```python
import math
import jax, jax.numpy as jnp
from jax import lax
import numpy as np

D_MODEL = 1024
BATCH = 1
SEQ = 256
DEPTH = 1

MOBA_HEAD_DIM = 64
MOBA_HEADS = (D_MODEL // 2) // MOBA_HEAD_DIM
MOBA_WIDTH = MOBA_HEADS * MOBA_HEAD_DIM
MOBA_BLOCK = 256
MOBA_TOPK = 3
Q_BLOCK = 128
GLA_HEADS = 4
GLA_VAL_DIM = (D_MODEL // 2) // GLA_HEADS
GLA_KEY_DIM = GLA_VAL_DIM // 2
GLA_VWIDTH = GLA_HEADS * GLA_VAL_DIM
GLA_KWIDTH = GLA_HEADS * GLA_KEY_DIM
GLA_GATE_RANK = 16
GLA_GATE_TAU = 16.0
GLA_CHUNK = 64
MIX_WIDTH = MOBA_WIDTH + GLA_VWIDTH
IN_COLS = 3 * MOBA_WIDTH + 2 * GLA_KWIDTH + 2 * GLA_VWIDTH + GLA_GATE_RANK
D_FF = 256 * ((8 * D_MODEL // 3 + 255) // 256)
CONV_WIDTH = 3
ROPE_THETA = 10000.0
EPS = 1e-6


def rms_norm(x, g):
    xf = x.astype(jnp.float32)
    y = xf * lax.rsqrt(jnp.mean(xf * xf, axis=-1, keepdims=True) + EPS)
    return (y * g.astype(jnp.float32)).astype(x.dtype)

def rope(t, pos):
    hd = t.shape[-1]
    inv_freq = 1.0 / (ROPE_THETA ** (jnp.arange(0, hd, 2, dtype=jnp.float32) / hd))
    ang = pos.astype(jnp.float32)[:, None] * inv_freq[None, :]
    cos = jnp.cos(ang).astype(t.dtype)
    sin = jnp.sin(ang).astype(t.dtype)
    t1, t2 = t[..., : hd // 2], t[..., hd // 2:]
    return jnp.concatenate([t1 * cos - t2 * sin, t2 * cos + t1 * sin], axis=-1)

def moba_attention(q, k, v):
    B, H, S, hd = q.shape
    nb = -(-S // MOBA_BLOCK)
    n_sel = min(MOBA_TOPK, nb)
    pad = nb * MOBA_BLOCK - S
    padw = ((0, 0), (0, 0), (0, pad), (0, 0))
    kp = jnp.pad(k, padw).reshape(B, H, nb, MOBA_BLOCK, hd)
    vp = jnp.pad(v, padw).reshape(B, H, nb, MOBA_BLOCK, hd)
    k_mean = jnp.mean(kp, axis=3)
    q = q * (hd ** -0.5)
    n_qb = S // Q_BLOCK
    gather = jax.vmap(jax.vmap(lambda blocks, idx: blocks[idx]))
    block_ids = jnp.arange(nb)

    def one_query_block(c):
        q0 = c * Q_BLOCK
        qc = lax.dynamic_slice_in_dim(q, q0, Q_BLOCK, axis=2)
        own = q0 // MOBA_BLOCK
        qpos = q0 + jnp.arange(Q_BLOCK)
        gate = jnp.einsum('bhqd,bhnd->bhqn', qc, k_mean).astype(jnp.float32)
        gate = jnp.where((block_ids < own)[None, None, None, :], gate, -jnp.inf)
        top_s, top_i = lax.top_k(gate, n_sel)
        valid = top_s > -jnp.inf
        kg = gather(kp, top_i)
        vg = gather(vp, top_i)
        s_sel = jnp.einsum('bhqd,bhqnkd->bhqnk', qc, kg).astype(jnp.float32)
        s_sel = jnp.where(valid[..., None], s_sel, -jnp.inf)
        s_sel = s_sel.reshape(B, H, Q_BLOCK, n_sel * MOBA_BLOCK)
        k_own = lax.dynamic_index_in_dim(kp, own, axis=2, keepdims=False)
        v_own = lax.dynamic_index_in_dim(vp, own, axis=2, keepdims=False)
        kpos = own * MOBA_BLOCK + jnp.arange(MOBA_BLOCK)
        s_own = jnp.einsum('bhqd,bhkd->bhqk', qc, k_own).astype(jnp.float32)
        s_own = jnp.where(qpos[:, None] >= kpos[None, :], s_own, -jnp.inf)
        p = jax.nn.softmax(jnp.concatenate([s_sel, s_own], axis=-1), axis=-1).astype(v.dtype)
        p_sel = p[..., : n_sel * MOBA_BLOCK].reshape(B, H, Q_BLOCK, n_sel, MOBA_BLOCK)
        p_own = p[..., n_sel * MOBA_BLOCK:]
        return (jnp.einsum('bhqnk,bhqnkd->bhqd', p_sel, vg)
                + jnp.einsum('bhqk,bhkd->bhqd', p_own, v_own))

    out = lax.map(one_query_block, jnp.arange(n_qb))
    return out.transpose(1, 2, 0, 3, 4).reshape(B, H, S, hd)

def gla_attention(q, k, v, log_a):
    B, H, S, dk = q.shape
    dv = v.shape[-1]
    C = GLA_CHUNK
    nc = S // C
    f32 = jnp.float32

    def to_chunks(t):
        return t.astype(f32).reshape(B, H, nc, C, t.shape[-1]).transpose(2, 0, 1, 3, 4)

    qc = to_chunks(q * (dk ** -0.5))
    kc, vc = to_chunks(k), to_chunks(v)
    G = jnp.cumsum(to_chunks(log_a), axis=3)
    causal = jnp.tril(jnp.ones((C, C), dtype=bool))

    def step(state, inp):
        q_, k_, v_, G_ = inp
        diff = G_[:, :, :, None, :] - G_[:, :, None, :, :]
        decay = jnp.exp(jnp.where(causal[None, None, :, :, None], diff, -jnp.inf))
        A = jnp.einsum('bhtd,bhsd,bhtsd->bhts', q_, k_, decay)
        o = (jnp.einsum('bhts,bhsv->bhtv', A, v_)
             + jnp.einsum('bhtd,bhdv->bhtv', q_ * jnp.exp(G_), state))
        G_last = G_[:, :, -1:, :]
        state = (jnp.exp(G_last)[:, :, 0, :, None] * state
                 + jnp.einsum('bhsd,bhsv->bhdv', k_ * jnp.exp(G_last - G_), v_))
        return state, o

    state0 = jnp.zeros((B, H, dk, dv), f32)
    _, o = lax.scan(step, state0, (qc, kc, vc, G))
    return o.transpose(1, 2, 0, 3, 4).reshape(B, H, S, dv)

def causal_dwconv(h, w, b):
    S = h.shape[1]
    hp = jnp.pad(h, ((0, 0), (CONV_WIDTH - 1, 0), (0, 0)))
    return sum(w[j] * hp[:, j:j + S] for j in range(CONV_WIDTH)) + b

def split_heads(t, n_heads):
    B, S, W = t.shape
    return t.reshape(B, S, n_heads, W // n_heads).transpose(0, 2, 1, 3)

def merge_heads(t):
    B, H, S, d = t.shape
    return t.transpose(0, 2, 1, 3).reshape(B, S, H * d)

def first_inputs(seed: int = 0) -> dict:
    key = jax.random.key(seed)
    ks = jax.random.split(key, 16)
    f32 = jnp.float32
    D, L = D_MODEL, DEPTH
    nrm = lambda k, shape, fan: jax.random.normal(k, shape, f32) * (fan ** -0.5)
    return {
        "x": jax.random.normal(ks[0], (BATCH, SEQ, D), f32),
        "attn_norm_g": 1.0 + 0.02 * jax.random.normal(ks[1], (L, D), f32),
        "w_in": nrm(ks[2], (L, D, IN_COLS), D),
        "w_gate_up": nrm(ks[3], (L, GLA_GATE_RANK, GLA_KWIDTH), GLA_GATE_RANK),
        "b_gate": 0.1 * jax.random.normal(ks[4], (L, GLA_KWIDTH), f32),
        "gla_norm_g": 1.0 + 0.02 * jax.random.normal(ks[5], (L, GLA_HEADS, GLA_VAL_DIM), f32),
        "w_out": nrm(ks[6], (L, MIX_WIDTH, D), MIX_WIDTH),
        "ffn_norm_g": 1.0 + 0.02 * jax.random.normal(ks[7], (L, D), f32),
        "w_ffn_up": nrm(ks[8], (L, D, 2 * D_FF), D),
        "conv_w": nrm(ks[9], (L, CONV_WIDTH, 2 * D_FF), CONV_WIDTH),
        "conv_b": 0.02 * jax.random.normal(ks[10], (L, 2 * D_FF), f32),
        "w_ffn_down": nrm(ks[11], (L, D_FF, D), D_FF),
        "final_norm_g": 1.0 + 0.02 * jax.random.normal(ks[12], (D,), f32),
    }

def first_block(x, attn_norm_g, w_in, w_gate_up, b_gate, gla_norm_g, w_out,
              ffn_norm_g, w_ffn_up, conv_w, conv_b, w_ffn_down, final_norm_g):
    B, S, _ = x.shape
    pos = jnp.arange(S)
    o_mq = 0
    o_mk = o_mq + MOBA_WIDTH
    o_mv = o_mk + MOBA_WIDTH
    o_gq = o_mv + MOBA_WIDTH
    o_gk = o_gq + GLA_KWIDTH
    o_gv = o_gk + GLA_KWIDTH
    o_gr = o_gv + GLA_VWIDTH
    o_gg = o_gr + GLA_VWIDTH
    for l in range(DEPTH):
        xn = rms_norm(x, attn_norm_g[l])
        proj = xn @ w_in[l]
        mq = rope(split_heads(proj[..., o_mq:o_mk], MOBA_HEADS), pos)
        mk = rope(split_heads(proj[..., o_mk:o_mv], MOBA_HEADS), pos)
        mv = split_heads(proj[..., o_mv:o_gq], MOBA_HEADS)
        y_moba = merge_heads(moba_attention(mq, mk, mv))
        gq = split_heads(proj[..., o_gq:o_gk], GLA_HEADS)
        gk = split_heads(proj[..., o_gk:o_gv], GLA_HEADS)
        gv = split_heads(proj[..., o_gv:o_gr], GLA_HEADS)
        gr = proj[..., o_gr:o_gg]
        gate_lr = proj[..., o_gg:]
        log_a = jax.nn.log_sigmoid((gate_lr @ w_gate_up[l] + b_gate[l]).astype(jnp.float32)) / GLA_GATE_TAU
        og = gla_attention(gq, gk, gv, split_heads(log_a, GLA_HEADS))
        og = og * lax.rsqrt(jnp.mean(og * og, axis=-1, keepdims=True) + EPS)
        og = og * gla_norm_g[l].astype(jnp.float32)[None, :, None, :]
        y_gla = merge_heads(og).astype(x.dtype) * jax.nn.silu(gr)
        x = x + jnp.concatenate([y_moba, y_gla], axis=-1) @ w_out[l]
        hn = rms_norm(x, ffn_norm_g[l])
        h = causal_dwconv(hn @ w_ffn_up[l], conv_w[l], conv_b[l])
        h_gate, h_val = h[..., :D_FF], h[..., D_FF:]
        x = x + (jax.nn.silu(h_gate) * h_val) @ w_ffn_down[l]
    return rms_norm(x, final_norm_g)


MIX_WIDTH_2 = 256
CONV_K = 3
GMLP_GROUPS = 4
GMLP_CHUNK = 128
HEAD_DIM = 64
SB_HEADS = MIX_WIDTH_2 // HEAD_DIM
FOX_HEADS = MIX_WIDTH_2 // HEAD_DIM
N_BRANCH = 4
FFN_HIDDEN = -(-8 * D_MODEL // (3 * 256)) * 256
IN_SPLIT_SIZES = (MIX_WIDTH_2, MIX_WIDTH_2, MIX_WIDTH_2, 2 * MIX_WIDTH_2, MIX_WIDTH_2, MIX_WIDTH_2, MIX_WIDTH_2,
                  MIX_WIDTH_2, MIX_WIDTH_2, MIX_WIDTH_2, FOX_HEADS, N_BRANCH * D_MODEL)
N_IN = sum(IN_SPLIT_SIZES)


def _rms_norm(x, g):
    xf = x.astype(jnp.float32)
    y = xf * lax.rsqrt(jnp.mean(xf * xf, axis=-1, keepdims=True) + EPS)
    return (y * g.astype(jnp.float32)).astype(x.dtype)

def _layer_norm(x, g, b):
    xf = x.astype(jnp.float32)
    mu = jnp.mean(xf, axis=-1, keepdims=True)
    var = jnp.mean(jnp.square(xf - mu), axis=-1, keepdims=True)
    y = (xf - mu) * lax.rsqrt(var + EPS)
    return (y * g.astype(jnp.float32) + b.astype(jnp.float32)).astype(x.dtype)

def _split_heads(t, n_heads):
    b, s, _ = t.shape
    return t.reshape(b, s, n_heads, HEAD_DIM).transpose(0, 2, 1, 3)

def _merge_heads(t):
    b, h, s, d = t.shape
    return t.transpose(0, 2, 1, 3).reshape(b, s, h * d)

def _short_conv_mixer(b_gate, c_gate, xt, w_conv):
    xc = c_gate * xt
    y = lax.conv_general_dilated(
        xc, w_conv[:, None, :].astype(xc.dtype), window_strides=(1,),
        padding=[(CONV_K - 1, 0)], dimension_numbers=('NWC', 'WIO', 'NWC'),
        feature_group_count=MIX_WIDTH_2)
    return b_gate * y

def _spatial_gating_mixer(uv, w_s, b_s, ln_g, ln_b):
    u, v = jnp.split(jax.nn.gelu(uv), 2, axis=-1)
    v = _layer_norm(v, ln_g, ln_b)
    bsz, s, _ = v.shape
    v = v.reshape(bsz, s // GMLP_CHUNK, GMLP_CHUNK, GMLP_GROUPS, MIX_WIDTH_2 // GMLP_GROUPS)
    w_causal = jnp.tril(w_s).astype(v.dtype)
    mixed = jnp.einsum('gts,bcsge->bctge', w_causal, v) + b_s.T[None, None, :, :, None].astype(v.dtype)
    return u * mixed.reshape(bsz, s, MIX_WIDTH_2)

def _stick_breaking_attention(q, k, v):
    seq = q.shape[2]
    scale = HEAD_DIM ** -0.5
    outs = []
    for i in range(seq // Q_BLOCK):
        start, end = i * Q_BLOCK, (i + 1) * Q_BLOCK
        z = jnp.einsum('bhqd,bhkd->bhqk', q[:, :, start:end], k[:, :, :end]).astype(jnp.float32) * scale
        q_pos = start + jnp.arange(Q_BLOCK)[:, None]
        k_pos = jnp.arange(end)[None, :]
        strict = k_pos < q_pos
        log_1m_beta = jnp.where(strict, jax.nn.log_sigmoid(-z), 0.0)
        later = lax.cumsum(log_1m_beta, axis=3, reverse=True) - log_1m_beta
        w = jnp.where(strict, jnp.exp(jax.nn.log_sigmoid(z) + later), 0.0)
        outs.append(jnp.einsum('bhqk,bhkd->bhqd', w.astype(v.dtype), v[:, :, :end]))
    return jnp.concatenate(outs, axis=2)

def _forgetting_attention(q, k, v, log_f_cum):
    seq = q.shape[2]
    scale = HEAD_DIM ** -0.5
    neg = jnp.finfo(jnp.float32).min
    outs = []
    for i in range(seq // Q_BLOCK):
        start, end = i * Q_BLOCK, (i + 1) * Q_BLOCK
        logits = jnp.einsum('bhqd,bhkd->bhqk', q[:, :, start:end], k[:, :, :end]).astype(jnp.float32) * scale
        logits = logits + log_f_cum[:, :, start:end, None] - log_f_cum[:, :, None, :end]
        causal = jnp.arange(end)[None, :] <= (start + jnp.arange(Q_BLOCK)[:, None])
        p = jax.nn.softmax(jnp.where(causal, logits, neg), axis=-1)
        outs.append(jnp.einsum('bhqk,bhkd->bhqd', p.astype(v.dtype), v[:, :, :end]))
    return jnp.concatenate(outs, axis=2)

def _mixer_block(xn, w_in, w_conv, w_s, b_s, ln_g, ln_b, q_norm_g, k_norm_g, b_f, w_branch, w_out):
    bsz, s, _ = xn.shape
    proj = xn @ w_in
    idx, acc = [], 0
    for size in IN_SPLIT_SIZES[:-1]:
        acc += size
        idx.append(acc)
    (cb, cc, cx, uv, sb_q, sb_k, sb_v, fx_q, fx_k, fx_v, f_raw, gate_raw) = jnp.split(proj, idx, axis=-1)

    y_a = _short_conv_mixer(cb, cc, cx, w_conv)
    y_b = _spatial_gating_mixer(uv, w_s, b_s, ln_g, ln_b)
    y_c = _merge_heads(_stick_breaking_attention(
        _split_heads(sb_q, SB_HEADS), _split_heads(sb_k, SB_HEADS), _split_heads(sb_v, SB_HEADS)))
    fq = _rms_norm(_split_heads(fx_q, FOX_HEADS), q_norm_g)
    fk = _rms_norm(_split_heads(fx_k, FOX_HEADS), k_norm_g)
    log_f = jax.nn.log_sigmoid((f_raw + b_f).astype(jnp.float32)).transpose(0, 2, 1)
    y_d = _merge_heads(_forgetting_attention(fq, fk, _split_heads(fx_v, FOX_HEADS), lax.cumsum(log_f, axis=2)))

    ys = jnp.stack([y_a, y_b, y_c, y_d], axis=2)
    branches = jnp.einsum('bsnc,ncd->bsnd', ys, w_branch)
    gates = jax.nn.sigmoid(gate_raw.reshape(bsz, s, N_BRANCH, D_MODEL).astype(jnp.float32)).astype(xn.dtype)
    merged = jnp.sum(gates * branches, axis=2)
    return merged @ w_out

def _swiglu(x, w_in, w_out):
    g, u = jnp.split(x @ w_in, 2, axis=-1)
    return (jax.nn.silu(g) * u) @ w_out

def second_inputs(seed: int = 0) -> dict:
    key = jax.random.key(seed)
    ks = jax.random.split(key, 16)
    f32 = jnp.float32
    nrm = lambda k, shape: jax.random.normal(k, shape, f32)
    return {
        'x': nrm(ks[0], (BATCH, SEQ, D_MODEL)),
        'norm_mix_g': 1.0 + 0.05 * nrm(ks[1], (DEPTH, D_MODEL)),
        'w_in': nrm(ks[2], (DEPTH, D_MODEL, N_IN)) * D_MODEL ** -0.5,
        'w_conv': nrm(ks[3], (DEPTH, CONV_K, MIX_WIDTH_2)) * CONV_K ** -0.5,
        'w_spatial': nrm(ks[4], (DEPTH, GMLP_GROUPS, GMLP_CHUNK, GMLP_CHUNK)) * GMLP_CHUNK ** -0.5,
        'b_spatial': 1.0 + 0.1 * nrm(ks[5], (DEPTH, GMLP_GROUPS, GMLP_CHUNK)),
        'gmlp_ln_g': 1.0 + 0.05 * nrm(ks[6], (DEPTH, MIX_WIDTH_2)),
        'gmlp_ln_b': 0.02 * nrm(ks[7], (DEPTH, MIX_WIDTH_2)),
        'fox_q_norm_g': 1.0 + 0.05 * nrm(ks[8], (DEPTH, HEAD_DIM)),
        'fox_k_norm_g': 1.0 + 0.05 * nrm(ks[9], (DEPTH, HEAD_DIM)),
        'fox_forget_b': 2.0 + 0.5 * nrm(ks[10], (DEPTH, FOX_HEADS)),
        'w_branch': nrm(ks[11], (DEPTH, N_BRANCH, MIX_WIDTH_2, D_MODEL)) * MIX_WIDTH_2 ** -0.5,
        'w_out': nrm(ks[12], (DEPTH, D_MODEL, D_MODEL)) * D_MODEL ** -0.5,
        'norm_ffn_g': 1.0 + 0.05 * nrm(ks[13], (DEPTH, D_MODEL)),
        'w_ffn_in': nrm(ks[14], (DEPTH, D_MODEL, 2 * FFN_HIDDEN)) * D_MODEL ** -0.5,
        'w_ffn_out': nrm(ks[15], (DEPTH, FFN_HIDDEN, D_MODEL)) * FFN_HIDDEN ** -0.5,
    }

def second_block(x, norm_mix_g, w_in, w_conv, w_spatial, b_spatial, gmlp_ln_g, gmlp_ln_b,
              fox_q_norm_g, fox_k_norm_g, fox_forget_b, w_branch, w_out, norm_ffn_g,
              w_ffn_in, w_ffn_out):
    h = x
    for l in range(DEPTH):
        xn = _rms_norm(h, norm_mix_g[l])
        h = h + _mixer_block(xn, w_in[l], w_conv[l], w_spatial[l], b_spatial[l], gmlp_ln_g[l],
                             gmlp_ln_b[l], fox_q_norm_g[l], fox_k_norm_g[l], fox_forget_b[l],
                             w_branch[l], w_out[l])
        h = h + _swiglu(_rms_norm(h, norm_ffn_g[l]), w_ffn_in[l], w_ffn_out[l])
    return h


def setup_inputs(seed=0):
    out = dict(first_inputs(seed))
    for name, value in second_inputs(seed + 1).items():
        if name != "x":
            out[name + "_2"] = value
    return out


def reference(
    x, attn_norm_g, w_in, w_gate_up, b_gate, gla_norm_g, w_out, ffn_norm_g, w_ffn_up, conv_w,
    conv_b, w_ffn_down, final_norm_g, norm_mix_g_2, w_in_2, w_conv_2, w_spatial_2, b_spatial_2,
    gmlp_ln_g_2, gmlp_ln_b_2, fox_q_norm_g_2, fox_k_norm_g_2, fox_forget_b_2, w_branch_2,
    w_out_2, norm_ffn_g_2, w_ffn_in_2, w_ffn_out_2,
):
    x = first_block(
        x, attn_norm_g, w_in, w_gate_up, b_gate, gla_norm_g, w_out, ffn_norm_g, w_ffn_up,
        conv_w, conv_b, w_ffn_down, final_norm_g,
    )
    return second_block(
        x, norm_mix_g_2, w_in_2, w_conv_2, w_spatial_2, b_spatial_2, gmlp_ln_g_2, gmlp_ln_b_2,
        fox_q_norm_g_2, fox_k_norm_g_2, fox_forget_b_2, w_branch_2, w_out_2, norm_ffn_g_2,
        w_ffn_in_2, w_ffn_out_2,
    )


_drawn_inputs = setup_inputs


def setup_inputs(seed=0):
    import zlib

    import numpy as np

    out = dict(_drawn_inputs(seed))
    spreads = {}
    factors = {'gla_norm_g': 4.744,
     'ffn_norm_g': 3.013,
     'conv_b': 3.082,
     'gmlp_ln_g_2': 5.066,
     'gmlp_ln_b_2': 22.05,
     'fox_q_norm_g_2': 7.994,
     'fox_k_norm_g_2': 8.0,
     'b_spatial_2': 2.783,
     'norm_ffn_g_2': 2.798}
    for name, (base, spread) in spreads.items():
        noise = np.random.default_rng([zlib.crc32(name.encode()), seed]).standard_normal(out[name].shape)
        drawn = base * np.exp(spread * noise) if base else spread * noise
        out[name] = __import__('jax').numpy.asarray(drawn.astype(out[name].dtype))
    for name, factor in factors.items():
        out[name] = (out[name] * factor).astype(out[name].dtype)
    return out
```

```python
from contextlib import ExitStack

import numpy as np

import concourse.bass as bass
from concourse import mybir

ALU = mybir.AluOpType
ACT = mybir.ActivationFunctionType
F32 = mybir.dt.float32
F32R = mybir.dt.float32r
AX_X = mybir.AxisListType.X

P = 128
T = 256
TT = T // P
D = 1024
KT = D // P
EPS = 1e-6
NEG = -1e30
HD = 64
SCALE = HD ** -0.5
MOBA_W = 512
MOBA_H = MOBA_W // HD
GLA_H, GLA_K, GLA_V = 4, 64, 128
GLA_KW, GLA_VW, GATE_RANK, GATE_TAU = GLA_H * GLA_K, GLA_H * GLA_V, 16, 16.0
D_FF = 2816
MIX2 = 256
FOX_H = 4
N_BRANCH = 4

SLAB_W = 256
SLAB = KT * SLAB_W
FF = D_FF // SLAB_W
RAW = 3
SPLIT = 3

IN1 = ["gq", "gk", "gv0", "gv1", "gr0", "gr1", "mq0", "mq1", "mk0", "mk1", "mv0", "mv1"]
IN2 = ["cc", "cx", "cb", "sq", "sk", "sv", "fq", "fk", "fv", "u", "v"]
OUT1 = ["o2", "o3", "o0", "o1"]
EARLY = [f"e{n}_{m}" for n in range(2) for m in range(4)]
FFN_ORDER = ["g0", "v0"] + [n for f in range(1, FF) for n in (f"g{f}", f"v{f}", f"d{f - 1}")] + [f"d{FF - 1}"]
MERGE = [x for m in range(4) for x in ([f"l2_{m}", f"l3_{m}", f"m{m}"] + ([f"o{m - 1}"] if m else []))] + ["o3"]
STREAM = ([("in1", n) for n in IN1] + [("out1", n) for n in OUT1] + [("ffn1", n) for n in FFN_ORDER]
          + [("in2", n) for n in IN2] + [("in2", n) for n in EARLY]
          + [("mix2", n) for n in MERGE] + [("ffn2", n) for n in FFN_ORDER])
NS = len(STREAM)
AT = {key: i for i, key in enumerate(STREAM)}

GLA_LEVELS = [0, 128, 64, 32, 16, 8, 4, 2, 1]
MASKED_LEVELS = [n for n in GLA_LEVELS if n != 128]
C_ID, C_NEG, C_ROT, C_COS, C_SIN = 0, 128, 256, 384, 640
C_LEV = 896
C_HEAD = C_LEV + 128 * len(MASKED_LEVELS)
C_ONE = C_HEAD + 128
C_SUF = C_ONE + 128
C_STN = C_SUF + 128
C_TRI = C_STN + 128
C_SEL = C_TRI + 128
C_EPS = C_SEL + 4 * 256
C_W = C_EPS + 1

V_LAY = {}
_at = 0
for _n, _w in (("ng0", KT), ("ng1", KT), ("ng2", KT), ("ng3", KT), ("bgate", 2), ("glag", 4), ("cw", 3 * 2 * D_FF // P),
               ("cb", 2 * D_FF // P), ("wc2", 6), ("fqg", 1), ("fkg", 1), ("bf", 1), ("wup", 256), ("small", KT * 20),
               ("fg", D), ("lng", 256), ("lnb", 256), ("bsp", 256), ("wsp", 512)):
    V_LAY[_n] = (_at, _at + _w)
    _at += _w
V_W = _at
NCH = 2 * D_FF // P
SM_W = 144


def build(nc, x_in, slabs_in, vec_in, cst_in, out):
    with ExitStack() as ctx:
        def sb(name, shape, dt=F32):
            return ctx.enter_context(nc.sbuf_tensor(name, shape, dt))

        def sem(name):
            return ctx.enter_context(nc.semaphore(name))

        raw = sb("raw", [P, RAW, SLAB])
        hiw = sb("hiw", [P, SPLIT, SLAB], F32R)
        low = sb("low", [P, SPLIT, SLAB], F32R)
        xhi = sb("xhi", [P, KT, T], F32R)
        xlo = sb("xlo", [P, KT, T], F32R)
        yhi = sb("yhi", [P, KT, T], F32R)
        ylo = sb("ylo", [P, KT, T], F32R)
        h = sb("h", [P, TT, D])
        cst = sb("cst", [P, C_W])
        vec = sb("vec", [P, V_W])
        smh = sb("smh", [P, KT, SM_W], F32R)
        sml = sb("sml", [P, KT, SM_W], F32R)
        st = sb("st", [P, 64])
        arena_w = 14592
        arena = sb("arena", [P, arena_w])
        ps = ctx.enter_context(nc.psum_tensor("ps", [P, 8, 512], F32))

        class Arena:

            def __init__(self, at=0):
                self.at = at

            def take(self, *shape):
                n = int(np.prod(shape))
                v = arena[:, self.at:self.at + n]
                self.at += n
                assert self.at <= arena_w, self.at
                if len(shape) == 1:
                    return v
                names = "abcd"[:len(shape)]
                return v.rearrange(f"p ({' '.join(names)}) -> p {' '.join(names)}", **dict(zip(names, shape)))

        def C(at, n=128):
            return cst[:, at:at + n]

        def V(name):
            a, b = V_LAY[name]
            return vec[:, a:b]

        ident, ones = C(C_ID), C(C_ONE)
        eps = cst[:, C_EPS:C_EPS + 1]

        S = {}

        def s(name):
            if name not in S:
                S[name] = sem(name)
            return S[name]

        raw_full = [sem(f"raw_full{i}") for i in range(RAW)]
        hi_made = sem("hi_made")
        lo_made = sem("lo_made")
        slab_used = sem("slab_used")

        class Chain:

            def __init__(self, name):
                self.sem, self.n, self.i, self.per = sem(name), 0, None, 0

            def value(self):
                return self.n if self.i is None else self.n + self.i * self.per

            def step(self, eng, ins):
                ins.then_inc(self.sem, 1)
                self.n += 1
                eng.wait_ge(self.sem, self.value())

            def mark(self, ins):
                ins.then_inc(self.sem, 1)
                self.n += 1
                return self.value()

            def loop(self, i, per):
                self.i, self.per, self.start = i, per, self.n

            def end(self, times):
                assert self.n - self.start == self.per, (self.n - self.start, self.per)
                self.n, self.i = self.start + self.per * times, None

        tenants = [[] for _ in range(8)]
        lease = {}
        bank_full = [sem(f"bank_full{b}") for b in range(8)]
        bank_free = [sem(f"bank_free{b}") for b in range(8)]

        def tenant(name, bank, gives_back=1):
            filled, freed = sum(n > 0 for n in tenants[bank]), sum(tenants[bank])
            tenants[bank].append(gives_back)
            lease[name] = (bank, filled + 1, freed, gives_back)

        def bank(name):
            return ps[:, lease[name][0], :]

        def full(name):
            return bank_full[lease[name][0]], lease[name][1]

        def fills(name):
            return bank_full[lease[name][0]], 1

        def frees(name):
            return bank_free[lease[name][0]], 1

        def given_back(name):
            b, _, before, gives_back = lease[name]
            return bank_free[b], before + gives_back

        def take_bank(pe, name):
            b, _, n, _ = lease[name]
            if n:
                pe.wait_ge(bank_free[b], n)

        for q in range(4):
            tenant(f"n0_{q}", 4 + q, 2)
        tenant("gg", 0)
        tenant("gq", 2)
        tenant("z", 1, 2)
        tenant("gk", 3)
        for n, b in (("gv0", 4), ("gv1", 5), ("gr0", 6), ("gr1", 7)):
            tenant(n, b)
        for n, b, r in (("mq0", 0, 2), ("mq1", 1, 7), ("mk0", 0, 2), ("mk1", 1, 7)):
            tenant(n, b)
            tenant(n + "r", r)
        tenant("mv0", 0)
        tenant("mv1", 1)
        for i, L in enumerate(GLA_LEVELS):
            for par in range(2):
                tenant(f"lev{L}_{par}", 3 + (2 * i + par) % 4)
        for j in range(2):
            tenant(f"go{j}", j)
            tenant(f"gs{j}", 2)
        for hh in range(MOBA_H):
            tenant(f"ms{hh}", 3 + hh % 2)
            tenant(f"mt{hh}", 5 + hh % 2)
            if hh % 2 == 0:
                tenant(f"mo{hh // 2}", 7)
        for q in range(4):
            tenant(f"w1_{q}", q, 0)
        for q in range(4):
            tenant(f"n1_{q}", 4 + q, 2)
        FREE = {"ffn1": 2, "ffn2": 1}
        ffn_lease = {}

        def ffn_tenants(k):
            for q in range(4):
                tenant(f"{k}_acc{q}", q, 0)
            ffn_lease[k] = [(len(tenants[4 + b]), sum(tenants[4 + b])) for b in range(4)]
            for f in range(FF):
                for j in range(2):
                    tenants[4 + 2 * (f % 2) + j].append(FREE[k])

        ffn_tenants("ffn1")
        for q in range(4):
            tenant(f"n2_{q}", 4 + q, 2)
        tenant("cc", 0)
        tenant("cx", 1)
        tenant("cb", 2)
        tenant("sq", 3)
        tenant("sk", 0)
        tenant("sv", 1)
        tenant("fq", 4)
        tenant("fk", 5, 2)
        tenant("fqs", 6)
        tenant("fks", 7)
        tenant("f", 2)
        tenant("fv", 3)
        tenant("u", 0)
        tenant("v", 1, 2)
        for i, n in enumerate(EARLY):
            tenant(n, i % 2)
        for hh in range(4):
            tenant(f"ss{hh}", 2 + hh % 2)
            tenant(f"sr{hh}", 4 + hh % 2)
            if hh % 2 == 0:
                tenant(f"so{hh // 2}", 6)
        for hh in range(FOX_H):
            tenant(f"fs{hh}", 2 + hh % 2)
            tenant(f"ft{hh}", 4 + hh % 2)
            if hh % 2 == 0:
                tenant(f"fo{hh // 2}", 7)
        tenant("gm", 6)
        for m in range(4):
            tenant(f"l2_{m}", 6)
            tenant(f"l3_{m}", 7)
            for n in range(N_BRANCH):
                tenant(f"br{m}_{n}", 4 + n % 2)
        for q in range(4):
            tenant(f"w2_{q}", q, 0)
        for q in range(4):
            tenant(f"n3_{q}", 4 + q, 2)
        ffn_tenants("ffn2")

        def hidden(k, f, j):
            return ps[:, 4 + 2 * (f % 2) + j, :]

        def hidden_full(k, f, j, i=None):
            b = 2 * (f % 2) + j
            n = ffn_lease[k][b][0] + f // 2 + 1
            return bank_full[4 + b], n if i is None else n + i

        def hidden_free(k, f, j, i=None, done=True):
            b = 2 * (f % 2) + j
            n = ffn_lease[k][b][1] + (f // 2 + done) * FREE[k]
            return bank_free[4 + b], n if i is None else n + i * FREE[k]

        down_used = {"ffn1": sem("down_used1"), "ffn2": sem("down_used2")}
        proj_used = {"out1": sem("proj_used1"), "mix2": sem("proj_used2")}

        def consumed(n, i=None):
            stage, name = STREAM[n]
            if stage in FREE:
                f = int(name[1:])
                if name[0] == "d":
                    return down_used[stage], f + 1 if i is None else f + 1 + 2 * i
                return hidden_full(stage, f, "gv".index(name[0]), i)
            if stage == "out1":
                return proj_used[stage], OUT1.index(name) + 1
            if stage == "mix2" and name[0] == "o":
                return proj_used[stage], int(name[1:]) + 1
            if stage == "mix2" and name[0] == "m":
                return full(f"br{name[1:]}_3")
            return full(name)

        def piece(at, *shape):
            n = int(np.prod(shape))
            assert at + n <= arena_w, (at, shape)
            v = arena[:, at:at + n]
            if len(shape) == 1:
                return v
            names = "abcd"[:len(shape)]
            return v.rearrange(f"p ({' '.join(names)}) -> p {' '.join(names)}", **dict(zip(names, shape)))

        xs = piece(0, TT, D)
        junk_act, junk_dve = piece(2048, D), piece(3072, D)
        Dl = [piece(512 * j, 2, T) for j in range(2)]
        Kl = [piece(1024 + 512 * j, 2, T) for j in range(2)]
        Ql = [piece(2048 + 512 * j, 2, T) for j in range(2)]
        zb, za, ze = (piece(3072 + 512 * j, 2, T) for j in range(3))
        El = [za, ze]
        tmpm = [piece(3072, 4, P), piece(4608, 4, P)]
        ggT = piece(5120, 256)
        gqT, gkT, G = (piece(5376 + 512 * j, 2, T) for j in range(3))
        gv = piece(6912, TT, 2, 256)
        grT = piece(7936, GLA_H, T)
        Acat = piece(8960, GLA_H, 3, P)
        qpre, mrot = piece(10496, 2, T), piece(11008, 2, T)
        qT, kT = piece(11520, 4, T), piece(12544, 4, T)
        mv = piece(13568, TT, 2, 256)
        osq = [Ql[0], Ql[1]]
        orr = [G, gqT]
        pex1 = [piece(384 * j, 384) for j in range(2)]
        pt1 = [piece(768 + 384 * j, 384) for j in range(2)]
        yb = [piece(4096 + 1024 * j, 4, T) for j in range(2)]
        sil = [piece(6144 + 512 * j, 512) for j in range(2)]
        gt = [piece(7168 + 512 * j, 512) for j in range(2)]
        sg = piece(0, 2, KT, T)
        cc, xc, yv = (piece(4096 + 512 * j, 2, T) for j in range(3))
        fsq = [piece(5632 + 512 * j, 2, T) for j in range(2)]
        zs = [piece(4096 + 384 * j, 384) for j in range(2)]
        ea = [piece(4864 + 384 * j, 384) for j in range(2)]
        Lt = [piece(5632 + 384 * j, 384) for j in range(2)]
        wt = [piece(6400 + 384 * j, 384) for j in range(2)]
        sgl = [piece(4096 + 1024 * j, 2, 512) for j in range(2)]
        sqT, skT = piece(7168, 2, T), piece(7680, 2, T)
        sv = piece(8192, TT, 256)
        fqT = piece(8704, 2, T)
        fkp = piece(9216, FOX_H, T)
        fv = piece(10240, TT, 256)
        F8, nF8 = piece(10752, T), piece(11008, T)
        uT, vt = piece(11264, 2, T), piece(11776, TT, 256)
        vn = piece(12288, TT, 256)
        frs = [piece(12800, 2, T), piece(13312, 2, T)]
        lsa, lse = piece(13824, T), piece(14080, T)
        pex2 = [piece(12800 + 384 * j, 384) for j in range(2)]
        pt2 = [piece(13568 + 384 * j, 384) for j in range(2)]
        macc = [piece(6144 + 512 * j, 512) for j in range(2)]
        mtmp = [piece(12800 + 512 * j, 512) for j in range(2)]
        onesT = piece(14336, T)
        mh_all, ml_all = (t[:, :, :].rearrange("p k c -> p (k c)")[:, 0:1024].rearrange("p (a b) -> p a b", a=4)
                          for t in (smh, sml))

        def merged(t, m):
            return t[:, :, :].rearrange("p k c -> p (k c)")[:, 512 * (m % 2):512 * (m % 2) + 512]

        def pv_signal(hh):
            name = f"mo{hh // 2}" if hh < 8 else f"fo{(hh - 8) // 2}"
            return fills(name) if hh % 2 else (s("pv_first"), 1)

        def pv_done(hh):
            name = f"mo{hh // 2}" if hh < 8 else f"fo{(hh - 8) // 2}"
            return full(name) if hh % 2 else (s("pv_first"), hh // 2 + 1)

        def stick_signal(i):
            return fills(f"so{i // 2}") if i % 2 else (s("stick_first"), 1)

        def stick_done(i):
            return full(f"so{i // 2}") if i % 2 else (s("stick_first"), i // 2 + 1)

        def halves(ap):
            return ap.rearrange("p (a b) -> p a b", b=128)[:, 0:3:2, :]

        block = ctx.enter_context(nc.Block())

        @block.sync
        def _(sp):
            sp.dma_start(h[:, :, :], x_in.rearrange("(t p) d -> p t d", p=P)).then_inc(s("x_in"), 16)
            sp.dma_start(cst[:, :], cst_in).then_inc(s("cst_in"), 16)
            sp.dma_start(vec[:, :], vec_in).then_inc(s("vec_in"), 16)
            for j in range(RAW):
                sp.dma_start(raw[:, j, :], slabs_in[j]).then_inc(raw_full[j], 16)
            with sp.Fori(1, NS // RAW) as i:
                for j in range(RAW):
                    sp.wait_ge(lo_made, i * RAW + (j + 1 - RAW))
                    sp.dma_start(raw[:, j, :], slabs_in[i * RAW + j]).then_inc(raw_full[j], 16)
            for n in range(NS // RAW * RAW, NS):
                sp.wait_ge(lo_made, n - RAW + 1)
                sp.dma_start(raw[:, n % RAW, :], slabs_in[n]).then_inc(raw_full[n % RAW], 16)
            sp.wait_ge(s("h_made"), 18)
            sp.dma_start(out.rearrange("(t p) d -> p t d", p=P), h[:, :, :]).then_inc(s("out_sent"), 16)
            sp.wait_ge(s("out_sent"), 16)

        @block.gpsimd
        def _(pool):
            pool.memset(smh[:, :, :].bitcast(F32), 0.0).then_inc(s("small_zero"), 1)
            pool.memset(sml[:, :, :].bitcast(F32), 0.0).then_inc(s("small_zero"), 1)
            pool.wait_ge(*given_back("gk"))
            for i, L in enumerate(GLA_LEVELS[1:]):
                pool.wait_ge(s("decay"), i + 1)
                if i >= 2:
                    pool.wait_ge(*full(f"lev{GLA_LEVELS[i - 1]}_1"))
                pool.tensor_tensor(Kl[i % 2], El[i % 2], gkT, ALU.mult).then_inc(s("keys_scaled"), 1)
            pool.wait_ge(s("rstd_made"), 4)
            pool.memset(fkp, 0.0).then_inc(s("fk_zero"), 1)

        @block.scalar
        def _(act):
            me = Chain("act_step")

            def rnd(n, i=None):
                act.wait_ge(raw_full[n % RAW], 16 * (n // RAW + 1) if i is None else 16 * (n // RAW + 1) + i * 32)
                if n >= SPLIT:
                    act.wait_ge(*consumed(n - SPLIT, i))
                act.activation(hiw[:, n % SPLIT, :], raw[:, n % RAW, :], ACT.Copy).then_inc(hi_made, 1)

            def norm_stats(q, h_made):
                if h_made:
                    act.wait_ge(s("h_made"), h_made)
                act.activation(junk_act, h[:, 0, :], ACT.Square,
                               accum_out=st[:, 2 * q:2 * q + 1]).then_inc(s("ssq_made"), 1)
                act.wait_ge(s("ssq_made"), 2 * q + 2)
                me.step(act, act.activation(st[:, 16 + 2 * q:18 + 2 * q], st[:, 2 * q:2 * q + 2], ACT.Ln,
                                            scale=1.0 / D, bias=eps))
                act.activation(st[:, 32 + 2 * q:34 + 2 * q], st[:, 16 + 2 * q:18 + 2 * q], ACT.Exp,
                               scale=-0.5).then_inc(s("rstd_made"), 1)

            def norm_turned(n):
                for kt in range(KT):
                    act.wait_ge(*full(f"n{n}_{kt // 2}"))
                    act.activation(xhi[:, kt, :], bank(f"n{n}_{kt // 2}")[:, kt % 2 * T:(kt % 2 + 1) * T], ACT.Copy,
                                   scale=V(f"ng{n}")[:, kt:kt + 1]).then_inc(s("xhi_made"), 1)

            def evacuate(name, dst, func=ACT.Copy, scale=1.0):
                act.wait_ge(*full(name))
                src = bank(name)
                if len(dst.shape) == 3:
                    src = src.rearrange("p (a b) -> p a b", a=dst.shape[1])
                return act.activation(dst, src, func, scale=scale).then_inc(*frees(name))

            act.wait_ge(s("x_in"), 16)
            act.wait_ge(s("cst_in"), 16)
            norm_stats(0, 0)
            act.wait_ge(s("vec_in"), 16)
            act.wait_ge(s("small_zero"), 2)
            small = V("small").rearrange("p (k c) -> p k c", k=KT)
            act.activation(smh[:, :, 0:20], small, ACT.Copy).then_inc(s("small_hi"), 1)
            rnd(0)
            norm_turned(0)
            rnd(1)
            rnd(2)
            act.wait_ge(*full("gg"))
            act.activation(ggT[0:GATE_RANK, :], bank("gg")[0:GATE_RANK, 0:T], ACT.Copy).then_inc(*frees("gg"))
            rnd(3)
            evacuate("gq", gqT, scale=SCALE)
            act.wait_ge(*full("z"))
            for c in range(2):
                act.activation(zb[:, c, :], bank("z")[:, c * T:(c + 1) * T], ACT.Identity,
                               bias=V("bgate")[:, c:c + 1]).then_inc(*frees("z"))
            act.wait_ge(*given_back("z"))
            me.step(act, act.activation(za, zb, ACT.Abs))
            me.step(act, act.activation(ze, za, ACT.Exp, scale=-1.0))
            act.activation(za, ze, ACT.Ln, bias=1.0).then_inc(s("z_ln"), 1)
            rnd(4)
            evacuate("gk", gkT)
            rnd(5)

            def decay(i):
                act.wait_ge(s("level_diff"), i + 1)
                if i >= 2:
                    act.wait_ge(s("queries_scaled"), i - 1)
                    act.wait_ge(s("keys_scaled"), i - 1)
                act.activation(El[i % 2], Dl[i % 2], ACT.Exp, scale=1.0 / GATE_TAU).then_inc(s("decay"), 1)

            def diag01():
                for par in range(2):
                    act.wait_ge(*full(f"lev128_{par}"))
                    act.activation(Acat[:, par::2, 1, :], bank(f"lev128_{par}")[:, 0:256].rearrange(
                        "p (a b) -> p a b", a=2), ACT.Copy).then_inc(*frees(f"lev128_{par}"))

            decay(0)
            evacuate("gv0", gv[:, :, 0, :])
            rnd(6)
            decay(1)
            evacuate("gv1", gv[:, :, 1, :])
            rnd(7)
            evacuate("gr0", grT[:, 0:2, :], ACT.Silu)
            rnd(8)
            evacuate("gr1", grT[:, 2:4, :], ACT.Silu)
            rnd(9)
            decay(2)
            for i, n in enumerate(("mq0", "mq1", "mk0", "mk1")):
                if i:
                    act.wait_ge(s("roped"), i)
                evacuate(n, qpre)
                rnd(10 + i)
                if i == 0:
                    diag01()
                if i >= 1:
                    decay(2 + i)
            evacuate("mv0", mv[:, :, 0, :])
            rnd(14)
            decay(6)
            evacuate("mv1", mv[:, :, 1, :])
            decay(7)

            for j in range(2):
                act.wait_ge(*full(f"go{j}"))
                act.activation(osq[j], bank(f"go{j}").rearrange("p (a b) -> p a b", a=2),
                               ACT.Square).then_inc(s("o_sq"), 1)

            def softmax_head(hh, pre, pex):
                act.wait_ge(s("max_made"), hh + 1)
                c = 48 + 8 * (hh % 2)
                if hh >= 2:
                    act.wait_ge(*full(turned_name(hh - 2)))
                act.activation(pex[hh % 2][:, 0:128], bank(f"{pre}{hh % 8}")[:, 0:128], ACT.Exp, scale=SCALE,
                               bias=st[:, c:c + 1], accum_out=st[:, c + 2:c + 3]).then_inc(s("exp_made"), 1)
                act.activation(pex[hh % 2][:, 128:384], bank(f"{pre}{hh % 8}")[:, 128:384], ACT.Exp, scale=SCALE,
                               bias=st[:, c + 1:c + 2], accum_out=st[:, c + 3:c + 4])\
                   .then_inc(*frees(f"{pre}{hh % 8}"))

            def turned_name(hh):
                return f"mt{hh}" if hh < 8 else f"ft{hh - 8}"

            def heads(first, n, pre, turn, pex, pt, outn, ychunk, between=None):
                softmax_head(first, pre, pex)
                for i in range(n):
                    if i + 1 < n:
                        softmax_head(first + i + 1, pre, pex)
                    if between:
                        between(i)
                    act.wait_ge(*full(f"{turn}{i}"))
                    if i >= 2:
                        act.wait_ge(*pv_done(first + i - 2))
                    act.activation(pt[i % 2], bank(f"{turn}{i}")[:, 0:384], ACT.Copy).then_inc(*frees(f"{turn}{i}"))
                    if i >= 2 and i % 2 == 0:
                        head_out(f"{outn}{i // 2 - 1}", ychunk + i // 2 - 1)
                head_out(f"{outn}{n // 2 - 1}", ychunk + n // 2 - 1)

            def head_out(name, chunk):
                act.wait_ge(*full(name))
                act.activation(yhi[:, chunk, :], bank(name)[:, 0:T], ACT.Copy).then_inc(s("head_hi"), 1)

            def gla_norm(j):
                act.wait_ge(*full(f"gs{j}"))
                act.activation(orr[j], bank(f"gs{j}").rearrange("p (a b) -> p a b", a=2), ACT.Ln,
                               scale=1.0 / GLA_V, bias=eps).then_inc(*frees(f"gs{j}"))
                act.wait_ge(*given_back(f"gs{j}"))
                act.activation(orr[j], orr[j], ACT.Exp, scale=-0.5).then_inc(s("o_rstd"), 1)

            def gla_hi(j):
                act.wait_ge(s("gy_made"), j + 1)
                act.activation(yhi[:, 4 + 2 * j:6 + 2 * j, :], orr[j], ACT.Copy).then_inc(s("gy_hi"), 1)

            def between_moba(i):
                if i in (0, 1):
                    gla_norm(i)
                if i in (2, 3):
                    gla_hi(i - 2)

            heads(0, MOBA_H, "ms", "mt", pex1, pt1, "mo", 0, between_moba)
            first_ffn = AT[("ffn1", "g0")]
            for n in range(15, first_ffn + 3):
                rnd(n)
            norm_stats(1, 4)
            norm_turned(1)

            def ffn_step(k, f, i=None):
                b = AT[(k, "g0")]
                splits = [b + 3] if f == 0 else [b + 4 + 3 * (f - 1) + j for j in range(3)]
                splits = [n for n in splits if n < NS]
                par = f % 2
                for j in range(2):
                    if j < len(splits):
                        rnd(splits[j], i)
                    if j == 1 or len(splits) < 2:
                        for n in splits[2:]:
                            rnd(n, i)
                    act.wait_ge(*hidden_full(k, f, j, i))
                    if k == "ffn1":
                        for c in range(2):
                            ch = j * (NCH // 2) + 2 * f + c
                            if i is None:
                                sc, bi = V("cw")[:, 2 * NCH + ch:2 * NCH + ch + 1], V("cb")[:, ch:ch + 1]
                            else:
                                sc = vec[:, bass.ds(V_LAY["cw"][0] + 2 * NCH + ch + 4 * i, 1)]
                                bi = vec[:, bass.ds(V_LAY["cb"][0] + ch + 4 * i, 1)]
                            act.activation(yb[par][:, 2 * j + c, :], hidden(k, f, j)[:, c * T:(c + 1) * T],
                                           ACT.Identity, scale=sc, bias=bi).then_inc(s("tap2"), 1)
                    elif j == 0:
                        act.activation(sil[par], hidden(k, f, 0), ACT.Silu).then_inc(hidden_free(k, f, 0)[0], 1)
                if k == "ffn1":
                    act.wait_ge(*hidden_free(k, f, 0, i))
                    act.activation(sil[par], yb[par][:, 0:2, :].rearrange("p a b -> p (a b)"),
                                   ACT.Silu).then_inc(s("silu_made"), 1)
                    act.wait_ge(s("gated"), f + 1 if i is None else f + 1 + 2 * i)
                else:
                    act.wait_ge(*hidden_free(k, f, 1, i))
                if f >= 2:
                    act.wait_ge(down_used[k], f - 1 if i is None else f - 1 + 2 * i)
                act.activation(yhi[:, 2 * par:2 * par + 2, :].rearrange("p a b -> p (a b)"), gt[par],
                               ACT.Copy).then_inc(s(f"g_hi_{k}"), 1)

            def ffn(k):
                ffn_step(k, 0)
                ffn_step(k, 1)
                with act.Fori(0, (FF - 3) // 2) as i:
                    ffn_step(k, 2, i)
                    ffn_step(k, 3, i)
                ffn_step(k, FF - 1)

            ffn("ffn1")
            b2 = AT[("in2", "cc")]
            rnd(b2 + 1)
            rnd(b2 + 2)
            norm_stats(2, 8)
            norm_stats(3, 10)
            norm_turned(2)

            evacuate("cc", cc)
            rnd(b2 + 3)
            rnd(b2 + 4)
            act.wait_ge(*given_back("cx"))
            for c in range(2):
                act.activation(yv[:, c, :], xc[:, c, :], ACT.Copy, scale=V("wc2")[:, 4 + c:5 + c]).then_inc(s("yv_tap"), 1)
            act.wait_ge(*full("cb"))
            rnd(b2 + 5)

            def y_hi(k, chunk, src, wait):
                act.wait_ge(*wait)
                act.activation(yhi[:, chunk:chunk + 2, :], src, ACT.Copy).then_inc(s(f"y_hi{k}"), 1)

            y_hi("a", 0, yv, given_back("cb"))
            evacuate("sq", sqT)
            rnd(b2 + 6)
            evacuate("sk", skT)
            rnd(b2 + 7)
            evacuate("sv", sv)
            rnd(b2 + 8)
            for j, n in enumerate(("fq", "fk")):
                act.wait_ge(*full(n))
                act.activation(fsq[j], bank(n).rearrange("p (a b) -> p a b", a=2), ACT.Square).then_inc(s("f_sq"), 1)
                rnd(b2 + 9 + j)
            for j in range(2):
                act.wait_ge(*full(("fqs", "fks")[j]))
                act.activation(frs[j], bank(("fqs", "fks")[j]).rearrange("p (a b) -> p a b", a=2), ACT.Ln,
                               scale=1.0 / HD, bias=eps).then_inc(*frees(("fqs", "fks")[j]))
                act.wait_ge(*given_back(("fqs", "fks")[j]))
                act.activation(frs[j], frs[j], ACT.Exp, scale=-0.5).then_inc(s("f_rstd"), 1)
            act.wait_ge(*full("f"))
            act.activation(F8, bank("f")[:, 0:T], ACT.Identity, bias=V("bf")).then_inc(*frees("f"))
            act.wait_ge(*given_back("f"))
            me.step(act, act.activation(lsa, F8, ACT.Abs))
            me.step(act, act.activation(lse, lsa, ACT.Exp, scale=-1.0))
            act.activation(lsa, lse, ACT.Ln, bias=1.0).then_inc(s("f_ln"), 1)
            evacuate("fv", fv)
            rnd(b2 + 11)
            evacuate("u", uT, ACT.Gelu_apprx_tanh)
            rnd(b2 + 12)
            act.wait_ge(*full("v"))
            for tt in range(TT):
                act.activation(vt[:, tt, :], bank("v")[:, tt * 256:(tt + 1) * 256], ACT.Gelu_apprx_tanh,
                               accum_out=st[:, 42 + tt:43 + tt]).then_inc(*frees("v"))
            rnd(b2 + 13)

            def early_gate(i):
                n = EARLY[i]
                br, m = int(n[1]), int(n[3])
                evacuate(n, sg[:, br, 2 * m:2 * m + 2, :], ACT.Sigmoid)
                rnd(b2 + 14 + i)

            def layer_norm_rstd():
                act.wait_ge(s("v_var"), 1)
                me.step(act, act.activation(st[:, 46:48], st[:, 44:46], ACT.Ln, scale=1.0 / 256, bias=eps))
                act.activation(st[:, 30:32], st[:, 46:48], ACT.Exp, scale=-0.5).then_inc(s("v_rstd"), 1)

            layer_norm_rstd()

            def stick_a(i):
                act.wait_ge(*given_back(f"ss{i}"))
                me.step(act, act.activation(ea[i % 2], zs[i % 2], ACT.Abs))
                me.step(act, act.activation(wt[i % 2], ea[i % 2], ACT.Exp, scale=-1.0))
                act.activation(ea[i % 2], wt[i % 2], ACT.Ln, bias=1.0).then_inc(s("stick_ln"), 1)

            def stick_b(i):
                act.wait_ge(*given_back(f"sr{i}"))
                act.activation(wt[i % 2], zs[i % 2], ACT.Exp).then_inc(s("stick_w"), 1)

            for i in range(4):
                if i >= 2:
                    act.wait_ge(*stick_done(i - 2))
                stick_a(i)
                if i >= 1:
                    stick_b(i - 1)
                early_gate(i)
                if i == 3:
                    head_out("so0", 4)
            stick_b(3)
            head_out("so1", 5)

            def between_fox(i):
                early_gate(4 + i)

            heads(8, FOX_H, "fs", "ft", pex2, pt2, "fo", 6, between_fox)
            y_hi("b", 2, vt, (s("yb_made"), 1))

            base = AT[("mix2", "l2_0")]
            nxt = [base + 3]
            def rnd_to(n):
                while nxt[0] <= n and nxt[0] < NS:
                    rnd(nxt[0])
                    nxt[0] += 1
            nxt[0] = b2 + 22
            assert b2 + 22 == base + 3
            for m in range(4):
                if m >= 2:
                    act.wait_ge(s("merged"), m - 1)
                for j in range(2):
                    evacuate(f"l{2 + j}_{m}", sgl[m % 2][:, j, :], ACT.Sigmoid)
                    rnd_to(AT[("mix2", f"l{2 + j}_{m}")] + 3)
                rnd_to(AT[("mix2", f"m{m}")] + 3)
                act.wait_ge(s("merged"), m + 1)
                if m >= 2:
                    act.wait_ge(proj_used["mix2"], m - 1)
                act.activation(merged(smh, m), macc[m % 2], ACT.Copy).then_inc(s("merged_hi"), 1)
                if m:
                    rnd_to(AT[("mix2", f"o{m - 1}")] + 3)
            rnd_to(AT[("ffn2", "g0")] + 2)
            norm_stats(4, 14)
            norm_turned(3)
            ffn("ffn2")

        @block.vector
        def _(dve):
            me = Chain("dve_step")

            def res(n, i=None):
                dve.wait_ge(hi_made, n + 1 if i is None else n + 1 + 6 * i)
                dve.tensor_tensor(low[:, n % SPLIT, :], raw[:, n % RAW, :], hiw[:, n % SPLIT, :].bitcast(F32),
                                  ALU.subtract).then_inc(lo_made, 1)

            def norm_sums(q, waits):
                for w in waits:
                    dve.wait_ge(*w)
                dve.tensor_tensor_reduce(junk_dve, h[:, 1, :], h[:, 1, :], 1.0, 0.0, ALU.mult, ALU.add,
                                         st[:, 2 * q + 1:2 * q + 2]).then_inc(s("ssq_made"), 1)

            def norm_scaled(q):
                dve.wait_ge(s("rstd_made"), q + 1)
                for tt in range(TT):
                    dve.tensor_scalar(xs[:, tt, :], h[:, tt, :], st[:, 32 + 2 * q + tt:33 + 2 * q + tt], None,
                                      ALU.mult).then_inc(s("xs_made"), 1)

            def norm_turned(n):
                for kt in range(KT):
                    dve.wait_ge(s("xhi_made"), KT * n + (kt | 1) + 1)
                    dve.scalar_tensor_tensor(
                        out=xlo[:, kt, :], in0=bank(f"n{n}_{kt // 2}")[:, kt % 2 * T:(kt % 2 + 1) * T],
                        scalar=V(f"ng{n}")[:, kt:kt + 1], in1=xhi[:, kt, :].bitcast(F32), op0=ALU.mult,
                        op1=ALU.subtract).then_inc(*frees(f"n{n}_{kt // 2}"))

            def two(name):
                return bank(name).rearrange("p (a b) -> p a b", a=2)

            norm_sums(0, [(s("x_in"), 16)])
            norm_scaled(0)
            dve.wait_ge(s("small_hi"), 1)
            dve.tensor_tensor(sml[:, :, 0:20], V("small").rearrange("p (k c) -> p k c", k=KT),
                              smh[:, :, 0:20].bitcast(F32), ALU.subtract).then_inc(s("small_lo"), 1)
            dve.memset(onesT, 1.0).then_inc(s("ones_made"), 1)
            dve.tensor_tensor(V("wsp").rearrange("p (a b) -> p a b", a=4), V("wsp").rearrange("p (a b) -> p a b", a=4),
                              C(C_TRI).unsqueeze(1).broadcast_to([P, 4, P]), ALU.mult).then_inc(s("wsp_masked"), 1)
            res(0)
            norm_turned(0)
            res(1)
            res(2)
            res(3)
            dve.wait_ge(s("z_ln"), 1)
            dve.wait_ge(s("ones_made"), 1)
            me.step(dve, dve.scalar_tensor_tensor(out=zb, in0=zb, scalar=0.0, in1=za, op0=ALU.min, op1=ALU.subtract))
            for c in range(2):
                last = dve.tensor_tensor_scan(G[:, c, :], onesT, zb[:, c, :], 0.0, ALU.mult, ALU.add)
            me.step(dve, last)

            def diff(i):
                L = GLA_LEVELS[1 + i]
                if i >= 2:
                    dve.wait_ge(s("decay"), i - 1)
                nb = 2 * T // (2 * L)
                g = G.rearrange("p a b -> p (a b)").rearrange("p (n l) -> p n l", n=nb)
                d = Dl[i % 2].rearrange("p a b -> p (a b)").rearrange("p (n l) -> p n l", n=nb)
                mid = g[:, :, L - 1:L].broadcast_to([P, nb, L])
                dve.tensor_tensor(d[:, :, L:2 * L], g[:, :, L:2 * L], mid, ALU.subtract)
                dve.tensor_tensor(d[:, :, 0:L], mid, g[:, :, 0:L], ALU.subtract).then_inc(s("level_diff"), 1)

            def queries(i):
                dve.wait_ge(s("decay"), i + 1)
                dve.wait_ge(*given_back("gq"))
                if i >= 2:
                    dve.wait_ge(*full(f"lev{GLA_LEVELS[i - 1]}_1"))
                dve.tensor_tensor(Ql[i % 2], El[i % 2], gqT, ALU.mult).then_inc(s("queries_scaled"), 1)

            def level_scores(L):
                m = C(C_LEV + 128 * MASKED_LEVELS.index(L)).unsqueeze(1).broadcast_to([P, 4, P])
                for par in range(2):
                    dve.wait_ge(*full(f"lev{L}_{par}"))
                    src = bank(f"lev{L}_{par}").rearrange("p (a b) -> p a b", a=4)
                    if L == 0:
                        for blk in range(2):
                            ins = dve.tensor_tensor(Acat[:, par::2, 2 * blk, :], src[:, blk::2, :], m[:, 0:2, :],
                                                    ALU.mult)
                        ins.then_inc(*frees(f"lev{L}_{par}"))
                    else:
                        tmp = tmpm[par]
                        dve.tensor_tensor(tmp, src, m, ALU.mult).then_inc(*frees(f"lev{L}_{par}"))
                        dve.wait_ge(*given_back(f"lev{L}_{par}"))
                        for blk in range(2):
                            ins = dve.tensor_tensor(Acat[:, par::2, 2 * blk, :], Acat[:, par::2, 2 * blk, :],
                                                    tmp[:, blk::2, :], ALU.add)
                        ins.then_inc(s("scores_added"), 1)
                        dve.wait_ge(s("scores_added"), 2 * (MASKED_LEVELS.index(L) - 1) + par + 1)

            def rope(i, name, dst):
                dve.wait_ge(*given_back(name))
                me.step(dve, dve.tensor_tensor(dst, qpre, C(C_COS, T).unsqueeze(1).broadcast_to([P, 2, T]), ALU.mult))
                dve.wait_ge(*full(name + "r"))
                dve.tensor_tensor(mrot, two(name + "r"), C(C_SIN, T).unsqueeze(1).broadcast_to([P, 2, T]),
                                  ALU.mult).then_inc(*frees(name + "r"))
                dve.wait_ge(*given_back(name + "r"))
                dve.tensor_tensor(dst, dst, mrot, ALU.add).then_inc(s("roped"), 1)

            diff(0)
            diff(1)
            res(4)
            queries(0)
            res(5)
            res(6)
            diff(2)
            queries(1)
            res(7)
            level_scores(0)
            res(8)
            res(9)
            rope(0, "mq0", qT[:, 0:2, :])
            res(10)
            queries(2)
            diff(3)
            rope(1, "mq1", qT[:, 2:4, :])
            res(11)
            level_scores(64)
            queries(3)
            diff(4)
            rope(2, "mk0", kT[:, 0:2, :])
            res(12)
            level_scores(32)
            queries(4)
            diff(5)
            rope(3, "mk1", kT[:, 2:4, :])
            res(13)
            level_scores(16)
            queries(5)
            diff(6)
            res(14)
            level_scores(8)
            queries(6)
            diff(7)
            level_scores(4)
            queries(7)
            level_scores(2)
            level_scores(1)

            def masked_max(hh, name):
                dve.wait_ge(*full(name))
                me.step(dve, dve.tensor_tensor(halves(bank(name)[:, 0:384]), halves(bank(name)[:, 0:384]),
                                               C(C_NEG).unsqueeze(1).broadcast_to([P, 2, P]), ALU.add))
                c = 48 + 8 * (hh % 2)
                dve.tensor_reduce(st[:, c + 6:c + 7], bank(name)[:, 0:128], AX_X, ALU.max)
                me.step(dve, dve.tensor_reduce(st[:, c + 7:c + 8], bank(name)[:, 128:384], AX_X, ALU.max))
                if hh >= 2:
                    dve.wait_ge(s("probs_made"), hh - 1)
                dve.tensor_scalar(st[:, c:c + 2], st[:, c + 6:c + 8], -SCALE, None, ALU.mult).then_inc(s("max_made"), 1)

            def probs(hh, name, pex):
                c = 48 + 8 * (hh % 2)
                dve.wait_ge(s("exp_made"), hh + 1)
                dve.wait_ge(*given_back(name))
                me.step(dve, dve.reciprocal(st[:, c + 4:c + 6], st[:, c + 2:c + 4]))
                dve.tensor_scalar(pex[hh % 2][:, 0:128], pex[hh % 2][:, 0:128], st[:, c + 4:c + 5], None, ALU.mult)
                dve.tensor_scalar(pex[hh % 2][:, 128:384], pex[hh % 2][:, 128:384], st[:, c + 5:c + 6], None,
                                  ALU.mult).then_inc(s("probs_made"), 1)

            head_outs = [0]

            def head_lo(name, chunk):
                head_outs[0] += 1
                dve.wait_ge(s("head_hi"), head_outs[0])
                dve.tensor_tensor(ylo[:, chunk, :], bank(name)[:, 0:T], yhi[:, chunk, :].bitcast(F32),
                                  ALU.subtract).then_inc(*frees(name))

            def gla_norm(j):
                dve.wait_ge(s("o_rstd"), j + 1)
                dve.tensor_tensor(orr[j], two(f"go{j}"), orr[j], ALU.mult).then_inc(*frees(f"go{j}"))
                dve.wait_ge(*given_back(f"go{j}"))
                for c in range(2):
                    hh = 2 * j + c
                    ins = dve.scalar_tensor_tensor(out=orr[j][:, c, :], in0=orr[j][:, c, :],
                                                   scalar=V("glag")[:, hh:hh + 1], in1=grT[:, hh, :], op0=ALU.mult,
                                                   op1=ALU.mult)
                ins.then_inc(s("gy_made"), 1)

            def gla_lo(j):
                dve.wait_ge(s("gy_hi"), j + 1)
                dve.tensor_tensor(ylo[:, 4 + 2 * j:6 + 2 * j, :], orr[j], yhi[:, 4 + 2 * j:6 + 2 * j, :].bitcast(F32),
                                  ALU.subtract).then_inc(s("gy_lo"), 1)

            def heads(first, n, pre, pex, outn, ychunk, between):
                masked_max(first, f"{pre}0")
                for i in range(n):
                    if i + 1 < n:
                        masked_max(first + i + 1, f"{pre}{i + 1}")
                    probs(first + i, f"{pre}{i}", pex)
                    between(i)
                    if i >= 3 and i % 2:
                        head_lo(f"{outn}{i // 2 - 1}", ychunk + i // 2 - 1)
                head_lo(f"{outn}{n // 2 - 1}", ychunk + n // 2 - 1)

            def between_moba(i):
                if i in (1, 2):
                    gla_norm(i - 1)
                if i in (3, 4):
                    gla_lo(i - 3)

            heads(0, MOBA_H, "ms", pex1, "mo", 0, between_moba)

            def add_to_h(names, used, to):
                for n in range(*to[0]):
                    res(n)
                dve.wait_ge(*used)
                for q, name in enumerate(names):
                    dst = h[:, q // 2, q % 2 * 512:(q % 2 + 1) * 512]
                    dve.tensor_tensor(dst, bank(name), dst, ALU.add).then_inc(s("h_made"), 1)

            first_ffn = AT[("ffn1", "g0")]
            add_to_h([f"w1_{q}" for q in range(4)], (proj_used["out1"], 4), [(15, first_ffn + 3)])
            norm_sums(1, [(s("h_made"), 4)])
            norm_scaled(1)
            norm_turned(1)

            def ffn_step(k, f, i=None):
                b = AT[(k, "g0")]
                splits = [b + 3] if f == 0 else [b + 4 + 3 * (f - 1) + j for j in range(3)]
                splits = [n for n in splits if n < NS]
                par = f % 2
                for j in range(2):
                    if j < len(splits):
                        res(splits[j], i)
                    if j == 1 or len(splits) < 2:
                        for n in splits[2:]:
                            res(n, i)
                    if k == "ffn1":
                        for c in range(2):
                            ch = j * (NCH // 2) + 2 * f + c
                            t = 4 * f + 2 * j + 2
                            dve.wait_ge(s("tap2"), t if i is None else t + 8 * i)
                            dst, src = yb[par][:, 2 * j + c, :], hidden(k, f, j)[:, c * T:(c + 1) * T]
                            for tap in (1, 0):
                                o = 2 - tap
                                if i is None:
                                    w = V("cw")[:, tap * NCH + ch:tap * NCH + ch + 1]
                                else:
                                    w = vec[:, bass.ds(V_LAY["cw"][0] + tap * NCH + ch + 4 * i, 1)]
                                ins = dve.scalar_tensor_tensor(out=dst[:, o:], in0=src[:, 0:T - o], scalar=w,
                                                               in1=dst[:, o:], op0=ALU.mult, op1=ALU.add)
                                if tap:
                                    me.step(dve, ins)
                                else:
                                    ins.then_inc(hidden_free(k, f, j)[0], 1)
                if k == "ffn1":
                    dve.wait_ge(s("silu_made"), f + 1 if i is None else f + 1 + 2 * i)
                    dve.wait_ge(*hidden_free(k, f, 1, i))
                    dve.tensor_tensor(gt[par], sil[par], yb[par][:, 2:4, :].rearrange("p a b -> p (a b)"),
                                      ALU.mult).then_inc(s("gated"), 1)
                else:
                    dve.wait_ge(*hidden_free(k, f, 0, i))
                    dve.wait_ge(*hidden_full(k, f, 1, i))
                    dve.tensor_tensor(gt[par], hidden(k, f, 1), sil[par], ALU.mult).then_inc(hidden_free(k, f, 1)[0], 1)
                dve.wait_ge(s(f"g_hi_{k}"), f + 1 if i is None else f + 1 + 2 * i)
                dve.tensor_tensor(ylo[:, 2 * par:2 * par + 2, :].rearrange("p a b -> p (a b)"), gt[par],
                                  yhi[:, 2 * par:2 * par + 2, :].rearrange("p a b -> p (a b)").bitcast(F32),
                                  ALU.subtract).then_inc(s(f"g_lo_{k}"), 1)

            def ffn(k):
                ffn_step(k, 0)
                ffn_step(k, 1)
                with dve.Fori(0, (FF - 3) // 2) as i:
                    me.loop(i, 8 if k == "ffn1" else 0)
                    ffn_step(k, 2, i)
                    ffn_step(k, 3, i)
                    me.end((FF - 3) // 2)
                ffn_step(k, FF - 1)

            ffn("ffn1")
            b2 = AT[("in2", "cc")]
            add_to_h([f"ffn1_acc{q}" for q in range(4)], (down_used["ffn1"], FF), [(b2 + 1, b2 + 3)])
            norm_sums(2, [(s("h_made"), 8)])
            dve.wait_ge(s("rstd_made"), 3)
            for tt in range(TT):
                dve.scalar_tensor_tensor(out=h[:, tt, :], in0=h[:, tt, :], scalar=st[:, 36 + tt:37 + tt], in1=V("fg"),
                                         op0=ALU.mult, op1=ALU.mult).then_inc(s("h_made"), 1)
            norm_sums(3, [(s("h_made"), 10)])
            norm_scaled(3)
            norm_turned(2)

            dve.wait_ge(*given_back("cc"))
            res(b2 + 3)
            dve.wait_ge(*full("cx"))
            dve.tensor_tensor(xc, two("cx"), cc, ALU.mult).then_inc(*frees("cx"))
            dve.wait_ge(*given_back("cx"))
            res(b2 + 4)
            for c in range(2):
                dve.wait_ge(s("yv_tap"), c + 1)
                for tap in (1, 0):
                    o = 2 - tap
                    me.step(dve, dve.scalar_tensor_tensor(
                        out=yv[:, c, o:], in0=xc[:, c, 0:T - o], scalar=V("wc2")[:, 2 * tap + c:2 * tap + c + 1],
                        in1=yv[:, c, o:], op0=ALU.mult, op1=ALU.add))
            dve.wait_ge(*full("cb"))
            dve.tensor_tensor(yv, two("cb"), yv, ALU.mult).then_inc(*frees("cb"))
            res(b2 + 5)

            def y_lo(k, chunk, src):
                dve.wait_ge(s(f"y_hi{k}"), 1)
                dve.tensor_tensor(ylo[:, chunk:chunk + 2, :], src, yhi[:, chunk:chunk + 2, :].bitcast(F32),
                                  ALU.subtract).then_inc(s("y_lo"), 1)

            y_lo("a", 0, yv)
            for n in range(b2 + 6, b2 + 11):
                res(n)
            for j in range(2):
                dve.wait_ge(s("f_rstd"), j + 1)
                if j == 0:
                    dve.scalar_tensor_tensor(out=fqT, in0=two("fq"), scalar=V("fqg"), in1=frs[0], op0=ALU.mult,
                                             op1=ALU.mult).then_inc(*frees("fq"))
                else:
                    dve.wait_ge(s("fk_zero"), 1)
                    for par in range(2):
                        r = slice(64 * par, 64 * par + 64)
                        dve.scalar_tensor_tensor(out=fkp[r, par::2, :], in0=two("fk")[r], scalar=V("fkg")[r],
                                                 in1=frs[1][r], op0=ALU.mult, op1=ALU.mult).then_inc(*frees("fk"))
            dve.memset(onesT, 1.0)
            dve.wait_ge(s("f_ln"), 1)
            me.step(dve, dve.scalar_tensor_tensor(out=lse, in0=F8, scalar=0.0, in1=lsa, op0=ALU.min, op1=ALU.subtract))
            me.step(dve, dve.tensor_tensor_scan(lsa, onesT, lse, 0.0, ALU.mult, ALU.add))
            dve.tensor_scalar(F8, lsa, 1.0 / SCALE, None, ALU.mult)
            dve.tensor_scalar(nF8, lsa, -1.0 / SCALE, None, ALU.mult).then_inc(s("forget_made"), 1)
            res(b2 + 11)
            res(b2 + 12)
            dve.wait_ge(*given_back("v"))
            me.step(dve, dve.tensor_scalar(st[:, 28:30], st[:, 42:44], -1.0 / 256, None, ALU.mult))
            for tt in range(TT):
                ins = dve.tensor_scalar(vn[:, tt, :], vt[:, tt, :], st[:, 28 + tt:29 + tt], None, ALU.add)
            me.step(dve, ins)
            for tt in range(TT):
                ins = dve.tensor_tensor_reduce(vt[:, tt, :], vn[:, tt, :], vn[:, tt, :], 1.0, 0.0, ALU.mult, ALU.add,
                                               st[:, 44 + tt:45 + tt])
            ins.then_inc(s("v_var"), 1)
            res(b2 + 13)
            dve.wait_ge(s("v_rstd"), 1)
            for tt in range(TT):
                ins = dve.scalar_tensor_tensor(out=vn[:, tt, :], in0=vn[:, tt, :], scalar=st[:, 30 + tt:31 + tt],
                                               in1=V("lng"), op0=ALU.mult, op1=ALU.mult)
            me.step(dve, ins)
            dve.tensor_tensor(vn, vn, V("lnb").unsqueeze(1).broadcast_to([P, 2, 256]), ALU.add).then_inc(s("v_normed"), 1)

            def stick_scores(i):
                dve.wait_ge(*full(f"ss{i}"))
                if i >= 2:
                    dve.wait_ge(s("stick_w"), i - 1)
                z = bank(f"ss{i}")
                dve.scalar_tensor_tensor(out=halves(zs[i % 2]), in0=halves(z[:, 0:384]), scalar=SCALE,
                                         in1=C(C_STN).unsqueeze(1).broadcast_to([P, 2, P]), op0=ALU.mult, op1=ALU.add)
                dve.tensor_scalar(zs[i % 2][:, 128:256], z[:, 128:256], SCALE, None, ALU.mult).then_inc(*frees(f"ss{i}"))

            def stick_soft(i):
                dve.wait_ge(s("stick_ln"), i + 1)
                dve.scalar_tensor_tensor(out=Lt[i % 2], in0=zs[i % 2], scalar=0.0, in1=ea[i % 2], op0=ALU.max,
                                         op1=ALU.add).then_inc(s("stick_soft"), 1)

            def stick_arg(i):
                dve.wait_ge(*full(f"sr{i}"))
                dve.tensor_tensor(zs[i % 2], zs[i % 2], bank(f"sr{i}")[:, 0:384], ALU.subtract)\
                   .then_inc(*frees(f"sr{i}"))

            for i in range(4):
                stick_scores(i)
                if i >= 1:
                    stick_arg(i - 1)
                stick_soft(i)
                res(b2 + 14 + i)
            stick_arg(3)
            head_lo("so0", 4)
            head_lo("so1", 5)

            def between_fox(i):
                res(b2 + 18 + i)

            heads(8, FOX_H, "fs", pex2, "fo", 6, between_fox)
            dve.wait_ge(*full("gm"))
            gm = bank("gm").rearrange("p (a c b) -> p a c b", a=2, c=2)
            bsp = V("bsp").rearrange("p (a b) -> p a b", a=2)
            yb4 = vt.rearrange("p a (c b) -> p a c b", c=2)
            for a in range(2):
                ins = dve.tensor_tensor(yb4[:, a], gm[:, a], bsp[:, a, :].unsqueeze(1).broadcast_to([P, 2, P]), ALU.add)
            ins.then_inc(*frees("gm"))
            dve.wait_ge(*given_back("gm"))
            dve.tensor_tensor(vt, vt, uT, ALU.mult).then_inc(s("yb_made"), 1)
            y_lo("b", 2, vt)

            nxt = [b2 + 22]

            def res_to(n):
                while nxt[0] <= n and nxt[0] < NS:
                    res(nxt[0])
                    nxt[0] += 1

            for m in range(4):
                res_to(AT[("mix2", f"l3_{m}")] + 3)
                for n in range(N_BRANCH):
                    if n == N_BRANCH - 1:
                        res_to(AT[("mix2", f"m{m}")] + 2)
                    if n < 2:
                        gate = sg[:, n, 2 * m:2 * m + 2, :].rearrange("p a b -> p (a b)")
                    else:
                        dve.wait_ge(*given_back(f"l{n}_{m}"))
                        gate = sgl[m % 2][:, n - 2, :]
                    dve.wait_ge(*full(f"br{m}_{n}"))
                    dst = macc[m % 2] if n == 0 else mtmp[n % 2]
                    if m >= 2 and n == 0:
                        dve.wait_ge(s("merged_hi"), m - 1)
                    dve.tensor_tensor(dst, bank(f"br{m}_{n}"), gate, ALU.mult).then_inc(*frees(f"br{m}_{n}"))
                    if n:
                        dve.wait_ge(*given_back(f"br{m}_{n}"))
                        ins = dve.tensor_tensor(macc[m % 2], macc[m % 2], dst, ALU.add)
                        if n < N_BRANCH - 1:
                            me.step(dve, ins)
                        else:
                            ins.then_inc(s("merged"), 1)
                dve.wait_ge(s("merged_hi"), m + 1)
                dve.tensor_tensor(merged(sml, m), macc[m % 2],
                                  merged(smh, m).bitcast(F32), ALU.subtract).then_inc(s("merged_lo"), 1)
                res_to(AT[("mix2", f"m{m}")] + 3)
                if m:
                    res_to(AT[("mix2", f"o{m - 1}")] + 3)
            add_to_h([f"w2_{q}" for q in range(4)], (proj_used["mix2"], 4), [(nxt[0], AT[("ffn2", "g0")] + 3)])
            norm_sums(4, [(s("h_made"), 14)])
            norm_scaled(4)
            norm_turned(3)
            ffn("ffn2")
            add_to_h([f"ffn2_acc{q}" for q in range(4)], (down_used["ffn2"], FF), [(0, 0)])

        @block.tensor
        def _(pe):
            def turn(n):
                for q in range(4):
                    take_bank(pe, f"n{n}_{q}")
                    for kt in (2 * q, 2 * q + 1):
                        for tt in range(TT):
                            pe.wait_ge(s("xs_made"), 2 * n + tt + 1)
                            mm = pe.transpose(bank(f"n{n}_{q}")[:, kt % 2 * T + tt * P:kt % 2 * T + (tt + 1) * P],
                                              xs[:, tt, kt * P:(kt + 1) * P], ident)
                    mm.then_inc(*fills(f"n{n}_{q}"))
                for q in range(4):
                    pe.wait_ge(*given_back(f"n{n}_{q}"))

            def three(o, whi, wlo, mhi, mlo, start, stop):
                pe.matmul(o, whi, mhi, start=start, stop=False)
                pe.matmul(o, whi, mlo, start=False, stop=False)
                return pe.matmul(o, wlo, mhi, start=False, stop=stop)

            def slab_views(n, rows):
                return [t[:, n % SPLIT, :].rearrange("p (k c) -> p k c", k=rows) for t in (hiw, low)]

            def feature_major(o, n):
                hi, lo = slab_views(n, KT)
                for c in range(2):
                    for kt in range(KT):
                        cc_ = slice(c * P, (c + 1) * P)
                        mm = three(o[:, c * T:(c + 1) * T], hi[:, kt, cc_], lo[:, kt, cc_], xhi[:, kt, :],
                                   xlo[:, kt, :], kt == 0, kt == KT - 1)
                return mm

            def token_major(o, n):
                hi, lo = slab_views(n, KT)
                for tt in range(TT):
                    for kt in range(KT):
                        t_ = slice(tt * P, (tt + 1) * P)
                        mm = three(o[:, tt * 256:(tt + 1) * 256], xhi[:, kt, t_], xlo[:, kt, t_], hi[:, kt, :],
                                   lo[:, kt, :], kt == 0, kt == KT - 1)
                return mm

            def project(stage, name, how):
                n = AT[(stage, name)]
                take_bank(pe, name)
                pe.wait_ge(lo_made, n + 1)
                how(bank(name), n).then_inc(*fills(name))

            def small_product(name, cols):
                take_bank(pe, name)
                pe.wait_ge(s("small_lo"), 1)
                for kt in range(KT):
                    mm = three(bank(name)[:, 0:T], smh[:, kt, cols], sml[:, kt, cols], xhi[:, kt, :], xlo[:, kt, :],
                               kt == 0, kt == KT - 1)
                mm.then_inc(*fills(name))

            def out_slab(n, chunks, yh, yl, accs, first, last):
                hi, lo = slab_views(n, 2)
                for j in range(2):
                    for q in range(4):
                        tt, nh = q // 2, q % 2
                        mm = three(accs[q], yh[:, chunks[j], tt * P:(tt + 1) * P], yl[:, chunks[j], tt * P:(tt + 1) * P],
                                   hi[:, j, nh * 512:(nh + 1) * 512], lo[:, j, nh * 512:(nh + 1) * 512],
                                   first and j == 0, last and j == 1)
                return mm

            pe.wait_ge(s("cst_in"), 16)
            turn(0)
            small_product("gg", slice(0, 128))
            project("in1", "gq", feature_major)
            take_bank(pe, "z")
            pe.wait_ge(s("vec_in"), 16)
            pe.wait_ge(*given_back("gg"))
            for c in range(2):
                mm = pe.matmul(bank("z")[:, c * T:(c + 1) * T], V("wup")[0:GATE_RANK, c * P:(c + 1) * P],
                               ggT[0:GATE_RANK, :], start=True, stop=True)
            mm.then_inc(*fills("z"))
            project("in1", "gk", feature_major)

            def level(L):
                if L:
                    i = GLA_LEVELS.index(L) - 1
                    pe.wait_ge(s("queries_scaled"), i + 1)
                    pe.wait_ge(s("keys_scaled"), i + 1)
                    q_, k_ = Ql[i % 2], Kl[i % 2]
                else:
                    pe.wait_ge(*given_back("gq"))
                    pe.wait_ge(*given_back("gk"))
                    q_, k_ = gqT, gkT
                for par in range(2):
                    take_bank(pe, f"lev{L}_{par}")
                    o, r = bank(f"lev{L}_{par}"), slice(64 * par, 64 * par + 64)
                    for c in range(2):
                        if L == 128:
                            mm = pe.matmul(o[:, c * P:(c + 1) * P], k_[r, c, 0:P], q_[r, c, P:T], start=True, stop=True)
                        else:
                            for blk in range(2):
                                b = slice(blk * P, (blk + 1) * P)
                                mm = pe.matmul(o[:, (2 * c + blk) * P:(2 * c + blk + 1) * P], k_[r, c, b], q_[r, c, b],
                                               start=True, stop=True)
                    mm.then_inc(*fills(f"lev{L}_{par}"))

            def rotate(name):
                take_bank(pe, name + "r")
                pe.wait_ge(*given_back(name))
                pe.matmul(bank(name + "r"), C(C_ROT), qpre.rearrange("p a b -> p (a b)"), start=True, stop=True)\
                  .then_inc(*fills(name + "r"))

            for n in ("gv0", "gv1"):
                project("in1", n, token_major)
            for n in ("gr0", "gr1"):
                project("in1", n, feature_major)
            level(0)
            project("in1", "mq0", feature_major)
            rotate("mq0")
            level(128)
            project("in1", "mq1", feature_major)
            rotate("mq1")
            level(64)
            project("in1", "mk0", feature_major)
            rotate("mk0")
            level(32)
            project("in1", "mk1", feature_major)
            rotate("mk1")
            level(16)
            project("in1", "mv0", token_major)
            level(8)
            project("in1", "mv1", token_major)
            for L in (4, 2, 1):
                level(L)

            def softmax_scores(i, name):
                take_bank(pe, name)
                o = bank(name)
                r, c = slice(64 * (i % 2), 64 * (i % 2) + 64), i // 2
                pe.wait_ge(s("roped"), 4)
                pe.matmul(o[:, 0:P], qT[r, c, 0:P], kT[r, c, 0:P], start=True, stop=True)
                pe.matmul(o[:, P:3 * P], qT[r, c, P:T], kT[r, c, :], start=True, stop=True).then_inc(*fills(name))

            def turn_probs(hh, name, pex):
                take_bank(pe, name)
                pe.wait_ge(s("probs_made"), hh + 1)
                for j in range(3):
                    mm = pe.transpose(bank(name)[:, j * P:(j + 1) * P], pex[hh % 2][:, j * P:(j + 1) * P], ident)
                mm.then_inc(*fills(name))

            def values(i, hh, turned, name, pt, v0, v1, ready, signal=None):
                if i % 2 == 0:
                    take_bank(pe, name)
                pe.wait_ge(*ready)
                r = slice(64 * (i % 2), 64 * (i % 2) + 64)
                pe.matmul(bank(name)[r, 0:T], v0, pt[:, 0:T], start=True, stop=False)
                mm = pe.matmul(bank(name)[r, P:T], v1, pt[:, T:T + P], start=False, stop=True)
                return mm

            def moba_values(i):
                cols = slice((i % 4) * HD, (i % 4 + 1) * HD)
                mm = values(i, i, f"mt{i}", f"mo{i // 2}", pt1[i % 2], mv[:, 0, i // 4, cols], mv[:, 1, i // 4, cols],
                            given_back(f"mt{i}"))
                return mm

            pe.wait_ge(s("scores_added"), 2 * (len(MASKED_LEVELS) - 1))
            pe.wait_ge(*given_back("lev128_1"))
            for hh in range(GLA_H):
                name, o = f"go{hh // 2}", hh % 2 * T
                if hh % 2 == 0:
                    take_bank(pe, name)
                cols = slice((hh % 2) * GLA_V, (hh % 2 + 1) * GLA_V)
                pe.matmul(bank(name)[:, o:o + T], gv[:, 0, hh // 2, cols],
                          Acat[:, hh, 0:2, :].rearrange("p a b -> p (a b)"), start=True, stop=False)
                mm = pe.matmul(bank(name)[:, o + P:o + T], gv[:, 1, hh // 2, cols], Acat[:, hh, 2, :], start=False,
                               stop=True)
                if hh % 2:
                    mm.then_inc(*fills(name))

            def gla_sums(j):
                take_bank(pe, f"gs{j}")
                pe.wait_ge(s("o_sq"), j + 1)
                pe.matmul(bank(f"gs{j}"), ones, osq[j].rearrange("p a b -> p (a b)"), start=True, stop=True)\
                  .then_inc(*fills(f"gs{j}"))

            pe.wait_ge(*given_back("mv1"))
            softmax_scores(0, "ms0")
            for i in range(MOBA_H):
                if i + 1 < MOBA_H:
                    softmax_scores(i + 1, f"ms{i + 1}")
                if i < 2:
                    gla_sums(i)
                turn_probs(i, f"mt{i}", pex1)
                if i >= 1:
                    moba_values(i - 1).then_inc(*(pv_signal(i - 1)))
            moba_values(MOBA_H - 1).then_inc(*(pv_signal(MOBA_H - 1)))

            for c, n in enumerate(OUT1):
                k = int(n[1:])
                s_ = AT[("out1", n)]
                if c == 0:
                    for q in range(4):
                        take_bank(pe, f"w1_{q}")
                    pe.wait_ge(s("gy_lo"), 2)
                if k < 2:
                    pe.wait_ge(*given_back(f"mo{2 * k + 1}"))
                pe.wait_ge(lo_made, s_ + 1)
                out_slab(s_, (2 * k, 2 * k + 1), yhi, ylo, [bank(f"w1_{q}") for q in range(4)], c == 0,
                         c == len(OUT1) - 1)\
                    .then_inc(proj_used["out1"], 1)
            turn(1)

            def ffn_up(k, f, i=None):
                n0 = AT[(k, "g0")]
                n = n0 + f if f == 0 else n0 + 2 + 3 * (f - 1)
                for j in range(2):
                    if i is not None or f >= 2 or ffn_lease[k][2 * (f % 2) + j][1]:
                        pe.wait_ge(*hidden_free(k, f, j, i, done=False))
                    pe.wait_ge(lo_made, n + j + 1 if i is None else n + j + 1 + 6 * i)
                    feature_major(hidden(k, f, j), n + j).then_inc(hidden_full(k, f, j)[0], 1)

            def ffn_down(k, f, i=None):
                n = AT[(k, "d0")] + 3 * f if f < FF - 1 else AT[(k, f"d{FF - 1}")]
                if f == 0:
                    for q in range(4):
                        take_bank(pe, f"{k}_acc{q}")
                pe.wait_ge(s(f"g_lo_{k}"), f + 1 if i is None else f + 1 + 2 * i)
                pe.wait_ge(lo_made, n + 1 if i is None else n + 1 + 6 * i)
                par = f % 2
                out_slab(n, (2 * par, 2 * par + 1), yhi, ylo, [bank(f"{k}_acc{q}") for q in range(4)], f == 0,
                         f == FF - 1)\
                    .then_inc(down_used[k], 1)

            def ffn(k):
                ffn_up(k, 0)
                ffn_up(k, 1)
                ffn_down(k, 0)
                with pe.Fori(0, (FF - 3) // 2) as i:
                    for f in (2, 3):
                        ffn_up(k, f, i)
                        ffn_down(k, f - 1, i)
                ffn_up(k, FF - 1)
                ffn_down(k, FF - 2)
                ffn_down(k, FF - 1)

            ffn("ffn1")
            turn(2)
            for n in ("cc", "cx", "cb", "sq", "sk"):
                project("in2", n, feature_major)
            project("in2", "sv", token_major)
            project("in2", "fq", feature_major)
            project("in2", "fk", feature_major)
            small_product("f", slice(16, 144))
            for j in range(2):
                name = ("fqs", "fks")[j]
                take_bank(pe, name)
                pe.wait_ge(s("f_sq"), j + 1)
                pe.matmul(bank(name), C(C_HEAD), fsq[j].rearrange("p a b -> p (a b)"), start=True, stop=True)\
                  .then_inc(*fills(name))
            project("in2", "fv", token_major)
            project("in2", "u", feature_major)
            project("in2", "v", token_major)

            def stick_scores(i):
                name = f"ss{i}"
                take_bank(pe, name)
                pe.wait_ge(*given_back("sk"))
                o, r, c = bank(name), slice(64 * (i % 2), 64 * (i % 2) + 64), i // 2
                pe.matmul(o[:, 0:T], skT[r, c, 0:P], sqT[r, c, :], start=True, stop=True)
                pe.matmul(o[:, T:T + P], skT[r, c, P:T], sqT[r, c, P:T], start=True, stop=True).then_inc(*fills(name))

            def stick_sums(i):
                name = f"sr{i}"
                take_bank(pe, name)
                pe.wait_ge(s("stick_soft"), i + 1)
                pe.matmul(bank(name)[:, 0:3 * P], C(C_SUF), Lt[i % 2], start=True, stop=False)
                pe.matmul(bank(name)[:, P:2 * P], ones, Lt[i % 2][:, 2 * P:3 * P], start=False, stop=True)\
                  .then_inc(*fills(name))

            def stick_values(i):
                cols = slice(i * HD, (i + 1) * HD)
                mm = values(i, i, None, f"so{i // 2}", wt[i % 2], sv[:, 0, cols], sv[:, 1, cols], (s("stick_w"), i + 1))
                return mm

            stick_scores(0)
            for i in range(4):
                if i < 3:
                    stick_scores(i + 1)
                project("in2", EARLY[i], feature_major)
                stick_sums(i)
                if i >= 1:
                    stick_values(i - 1).then_inc(*stick_signal(i - 1))
            stick_values(3).then_inc(*stick_signal(3))

            def fox_scores(i):
                name = f"fs{i}"
                take_bank(pe, name)
                pe.wait_ge(*given_back("fk"))
                pe.wait_ge(s("forget_made"), 1)
                o, c = bank(name), i // 2
                sel = C(C_SEL + 256 * i, 256)
                for tt in range(TT):
                    t_ = slice(tt * P, (tt + 1) * P)
                    o_, n = (o[:, 0:P], P) if tt == 0 else (o[:, P:3 * P], T)
                    pe.matmul(o_, fqT[:, c, t_], fkp[:, i, 0:n], start=True, stop=False)
                    pe.matmul(o_, F8[:, t_], sel[:, 0:n], start=False, stop=False)
                    mm = pe.matmul(o_, sel[:, 0:P], nF8[:, 0:n], start=False, stop=True)
                mm.then_inc(*fills(name))

            def fox_values(i):
                cols = slice(i * HD, (i + 1) * HD)
                return values(i, 8 + i, None, f"fo{i // 2}", pt2[i % 2], fv[:, 0, cols], fv[:, 1, cols],
                              given_back(f"ft{i}"))

            fox_scores(0)
            for i in range(FOX_H):
                if i + 1 < FOX_H:
                    fox_scores(i + 1)
                project("in2", EARLY[4 + i], feature_major)
                turn_probs(8 + i, f"ft{i}", pex2)
                if i >= 1:
                    fox_values(i - 1).then_inc(*pv_signal(8 + i - 1))
            fox_values(3).then_inc(*pv_signal(11))
            take_bank(pe, "gm")
            pe.wait_ge(s("v_normed"), 1)
            wsp = V("wsp").rearrange("p (a b) -> p a b", a=4)
            for g in range(4):
                r = slice(64 * (g % 2), 64 * (g % 2) + 64)
                for c in range(2):
                    at = (g // 2) * T + c * P
                    mm = pe.matmul(bank("gm")[r, at:at + P], vn[:, c, g * 64:(g + 1) * 64], wsp[:, g, :], start=True,
                                   stop=True)
            mm.then_inc(*fills("gm"))

            def mix_out(m):
                n = AT[("mix2", f"o{m}")]
                if m == 0:
                    for q in range(4):
                        take_bank(pe, f"w2_{q}")
                pe.wait_ge(s("merged_lo"), m + 1)
                pe.wait_ge(lo_made, n + 1)
                out_slab(n, (2 * (m % 2), 2 * (m % 2) + 1), mh_all, ml_all, [bank(f"w2_{q}") for q in range(4)],
                         m == 0, m == 3)\
                    .then_inc(proj_used["mix2"], 1)

            for m in range(4):
                for j in range(2):
                    project("mix2", f"l{2 + j}_{m}", feature_major)
                n_ = AT[("mix2", f"m{m}")]
                pe.wait_ge(lo_made, n_ + 1)
                if m == 0:
                    pe.wait_ge(s("y_lo"), 2)
                    pe.wait_ge(*given_back("so1"))
                    pe.wait_ge(*given_back("fo1"))
                hi, lo = [t[:, n_ % SPLIT, :].rearrange("p (n k c) -> p n k c", n=4, k=2) for t in (hiw, low)]
                for n in range(N_BRANCH):
                    take_bank(pe, f"br{m}_{n}")
                    for c in range(2):
                        for k in range(2):
                            c_ = slice(c * P, (c + 1) * P)
                            mm = three(bank(f"br{m}_{n}")[:, c * T:(c + 1) * T], hi[:, n, k, c_], lo[:, n, k, c_],
                                       yhi[:, 2 * n + k, :], ylo[:, 2 * n + k, :], k == 0, k == 1)
                    mm.then_inc(*fills(f"br{m}_{n}"))
                if m:
                    mix_out(m - 1)
            mix_out(3)
            turn(3)
            ffn("ffn2")


_INS = ["x", "slabs", "vec", "cst"]


def constants():
    c = np.zeros((P, C_W), np.float32)
    i, j = np.arange(P)[:, None], np.arange(P)[None, :]
    c[:, C_ID:C_ID + P] = i == j
    c[:, C_NEG:C_NEG + P] = np.where(j > i, NEG, 0)
    half = HD // 2
    for k in range(P):
        if k % HD < half:
            c[k + half, C_ROT + k] = -1
        else:
            c[k - half, C_ROT + k] = 1
    freq = (1.0 / (np.float32(10000.0) ** (np.arange(0, HD, 2, dtype=np.float32) / np.float32(HD)))).astype(np.float32)
    ang = (np.arange(T, dtype=np.float32)[None, :] * freq[np.arange(P) % half][:, None]).astype(np.float32)
    c[:, C_COS:C_COS + T] = np.cos(ang)
    c[:, C_SIN:C_SIN + T] = np.sin(ang)
    for n, L in enumerate(MASKED_LEVELS):
        m = (i == j) if L == 0 else (i // (2 * L) == j // (2 * L)) & (i % (2 * L) < L) & (j % (2 * L) >= L)
        c[:, C_LEV + n * P:C_LEV + (n + 1) * P] = m
    c[:, C_HEAD:C_HEAD + P] = i // HD == j // HD
    c[:, C_ONE:C_ONE + P] = 1
    c[:, C_SUF:C_SUF + P] = i >= j
    c[:, C_STN:C_STN + P] = np.where(i >= j, NEG, 0)
    c[:, C_TRI:C_TRI + P] = i <= j
    for k in range(4):
        c[k, C_SEL + 256 * k:C_SEL + 256 * (k + 1)] = 1
    c[:, C_EPS] = EPS
    return c


def columns(w, at, n=SLAB_W):
    return w[:, at:at + n].reshape(KT, P, n).transpose(1, 0, 2)


def rows(w, at):
    return w[256 * at:256 * (at + 1)].reshape(2, P, D).transpose(1, 0, 2)


IN1_AT = {"mq0": 0, "mq1": 256, "mk0": 512, "mk1": 768, "mv0": 1024, "mv1": 1280, "gq": 1536, "gk": 1792, "gv0": 2048,
          "gv1": 2304, "gr0": 2560, "gr1": 2816}
IN2_AT = {"cb": 0, "cc": 256, "cx": 512, "u": 768, "v": 1024, "sq": 1280, "sk": 1536, "sv": 1792, "fq": 2048,
          "fk": 2304, "fv": 2560}
GATE_AT = 2820


def slab(stage, name, w):
    k = int(name[1:]) if name[1:].isdigit() else 0
    if stage == "in1":
        return columns(w["w_in"], IN1_AT[name])
    if stage == "in2":
        if name[0] == "e":
            return columns(w["w_in_2"], GATE_AT + D * int(name[1]) + 256 * int(name[3]))
        return columns(w["w_in_2"], IN2_AT[name])
    if stage == "out1":
        return rows(w["w_out"], k)
    if stage == "mix2":
        if name[0] == "l":
            return columns(w["w_in_2"], GATE_AT + D * int(name[1]) + 256 * int(name[3]))
        if name[0] == "o":
            return rows(w["w_out_2"], k)
        return w["w_branch_2"][:, :, 256 * k:256 * (k + 1)].reshape(4, 2, P, 256).transpose(2, 0, 1, 3)
    up, down = ("w_ffn_up", "w_ffn_down") if stage == "ffn1" else ("w_ffn_in_2", "w_ffn_out_2")
    if name[0] == "d":
        return rows(w[down], k)
    return columns(w[up], 256 * k + (D_FF if name[0] == "v" else 0))


def chunked(v):
    return v.reshape(-1, P).T


def small_inputs(w):
    v = np.zeros((P, V_W), np.float32)

    def put(name, a):
        lo, hi = V_LAY[name]
        v[0:a.shape[0], lo:hi] = a

    for n, name in enumerate(("attn_norm_g", "ffn_norm_g", "norm_mix_g_2", "norm_ffn_g_2")):
        put(f"ng{n}", chunked(w[name]))
    put("bgate", chunked(w["b_gate"]))
    put("glag", w["gla_norm_g"].T)
    put("cw", chunked(w["conv_w"]))
    put("cb", chunked(w["conv_b"]))
    put("wc2", chunked(w["w_conv_2"]))
    put("fqg", np.concatenate([w["fox_q_norm_g_2"]] * 2)[:, None])
    put("fkg", np.concatenate([w["fox_k_norm_g_2"]] * 2)[:, None])
    put("bf", w["fox_forget_b_2"][:, None])
    put("wup", w["w_gate_up"])
    small = np.concatenate([w["w_in"][:, 3072:3088], w["w_in_2"][:, 2816:2820]], axis=1)
    put("small", small.reshape(KT, P, 20).transpose(1, 0, 2).reshape(P, KT * 20))
    put("fg", np.broadcast_to(w["final_norm_g"], (P, D)))
    put("lng", np.broadcast_to(w["gmlp_ln_g_2"], (P, 256)))
    put("lnb", np.broadcast_to(w["gmlp_ln_b_2"], (P, 256)))
    put("bsp", np.repeat(w["b_spatial_2"].reshape(2, 2, 1, P), 64, axis=2).reshape(2, P, P).transpose(1, 0, 2)
        .reshape(P, 256))
    put("wsp", w["w_spatial_2"].transpose(2, 0, 1).reshape(P, 512))
    return v


def kernel(**inputs):
    import concourse.bacc as _bacc
    from concourse.bass_utils import run_bass_kernel_spmd as _run

    w = {}
    for name, a in inputs.items():
        a = np.asarray(a)
        w[name] = a if name == "final_norm_g" or name == "x" else a[0]
    arrays = {
        "in_x": np.ascontiguousarray(w["x"][0]),
        "in_slabs": np.stack([slab(stage, name, w).reshape(P, SLAB) for stage, name in STREAM]),
        "in_vec": small_inputs(w),
        "in_cst": constants(),
    }
    nc = _bacc.Bacc("TRN2", target_bir_lowering=False, num_devices=1)
    args = [nc.dram_tensor(n, a.shape, F32, kind="ExternalInput").ap() for n, a in arrays.items()]
    args.append(nc.dram_tensor("out_0", (T, D), F32, kind="ExternalOutput").ap())
    build(nc, *args)
    r = _run(nc, [arrays], core_ids=[0])
    return r.results[0]["out_0"].reshape(1, T, D)
```

```python
from contextlib import ExitStack

import numpy as np

import concourse.bass as bass
from concourse import mybir

ALU = mybir.AluOpType
ACT = mybir.ActivationFunctionType
F32 = mybir.dt.float32
F32R = mybir.dt.float32r
AX_X = mybir.AxisListType.X

P = 128
T = 256
TT = T // P
D = 1024
KT = D // P
EPS = 1e-6
NEG = -1e30
HD = 64
SCALE = HD ** -0.5
MOBA_W = 512
MOBA_H = MOBA_W // HD
GLA_H, GLA_K, GLA_V = 4, 64, 128
GLA_KW, GLA_VW, GATE_RANK, GATE_TAU = GLA_H * GLA_K, GLA_H * GLA_V, 16, 16.0
D_FF = 2816
MIX2 = 256
FOX_H = 4
N_BRANCH = 4

SLAB_W = 256
SLAB = KT * SLAB_W
FF = D_FF // SLAB_W
RAW = 3
SPLIT = 3

IN1 = ["gq", "gk", "mq0", "mk0", "mv0", "mq1", "mk1", "mv1", "gv0", "gv1", "gr0", "gr1"]
ROPED = ["mq0", "mk0", "mq1", "mk1"]
IN2 = ["sq", "sk", "sv", "fq", "fk", "fv", "cc", "cx", "cb", "u", "v"]
OUT1 = ["o0", "o2", "o3", "o1"]
EARLY = [f"e{n}_{m}" for n in range(2) for m in range(4)]
FFN_ORDER = (["g0", "v0"] + [n for f in range(1, FF - 2) for n in (f"g{f}", f"v{f}", f"d{f - 1}")]
             + [f"{x}{f}" for f in (FF - 2, FF - 1) for x in "gv"] + [f"d{f}" for f in range(FF - 3, FF)])
WARM = [12, 11, 19, 13]
FFN_PAIRS = (FF - 3) // 2 - 1
MERGE = [x for m in range(4) for x in ([f"l2_{m}", f"l3_{m}", f"m{m}"] + ([f"o{m - 1}"] if m else []))] + ["o3"]
STREAM = ([("in1", n) for n in IN1] + [("out1", n) for n in OUT1] + [("ffn1", n) for n in FFN_ORDER]
          + [("in2", n) for n in IN2] + [("in2", n) for n in EARLY]
          + [("mix2", n) for n in MERGE] + [("ffn2", n) for n in FFN_ORDER])
NS = len(STREAM)
AT = {key: i for i, key in enumerate(STREAM)}

GLA_LEVELS = [0, 128, 64, 32, 16, 8, 4, 2, 1]
LEVEL_SLAB = {n: max(2, i + 1) for i, n in enumerate(GLA_LEVELS)}
MASKED_LEVELS = [n for n in GLA_LEVELS if n != 128]
C_ID, C_EPS, C_MHALF = 0, 128, 129
C_FIRST = 132
C_NEG, C_ROT, C_COS, C_SIN = (C_FIRST + n for n in (0, 128, 256, 512))
C_LEV = C_FIRST + 768
C_HEAD = C_LEV + 128 * len(MASKED_LEVELS)
C_ONE = C_HEAD + 128
C_SUF = C_ONE + 128
C_STN = C_SUF + 128
C_TRI = C_STN + 128
C_SEL = C_TRI + 128
C_W = C_SEL + 8

V_LAY = {}
_at = 0
for _n, _w in (("ng0", KT), ("small", KT * 24), ("bgate", 2), ("wup", 256), ("ng1", KT), ("ng2", KT), ("ng3", KT),
               ("glag", 4), ("cw", 3 * 2 * D_FF // P), ("cb", 2 * D_FF // P), ("wc2", 6), ("fqg", 1), ("fkg", 1), ("bf", 1),
               ("fg", D), ("lng", 256), ("lnb", 256), ("bsp", 256), ("wsp", 512)):
    V_LAY[_n] = (_at, _at + _w)
    _at += _w
V_W = _at
V_FIRST = V_LAY["wup"][1]
NCH = 2 * D_FF // P
SM_W = 144


def build(nc, x_in, slabs_in, vec_in, cst_in, out):
    with ExitStack() as ctx:
        def sb(name, shape, dt=F32):
            return ctx.enter_context(nc.sbuf_tensor(name, shape, dt))

        def sem(name):
            return ctx.enter_context(nc.semaphore(name))

        raw = sb("raw", [P, RAW, SLAB])
        hiw = sb("hiw", [P, SPLIT, SLAB], F32R)
        low = sb("low", [P, SPLIT, SLAB], F32R)
        xhi = sb("xhi", [P, KT, T], F32R)
        xlo = sb("xlo", [P, KT, T], F32R)
        yhi = sb("yhi", [P, KT, T], F32R)
        ylo = sb("ylo", [P, KT, T], F32R)
        h = sb("h", [P, TT, D])
        cst = sb("cst", [P, C_W])
        vec = sb("vec", [P, V_W])
        smh = sb("smh", [P, KT, SM_W], F32R)
        sml = sb("sml", [P, KT, SM_W], F32R)
        st = sb("st", [P, 128])
        diag = sb("diag", [P, TT, P])
        zeros = sb("zeros", [P, P])
        arena_w = 15104
        arena = sb("arena", [P, arena_w])
        ps = ctx.enter_context(nc.psum_tensor("ps", [P, 8, 512], F32))

        class Arena:

            def __init__(self, at=0):
                self.at = at

            def take(self, *shape):
                n = int(np.prod(shape))
                v = arena[:, self.at:self.at + n]
                self.at += n
                assert self.at <= arena_w, self.at
                if len(shape) == 1:
                    return v
                names = "abcd"[:len(shape)]
                return v.rearrange(f"p ({' '.join(names)}) -> p {' '.join(names)}", **dict(zip(names, shape)))

        def C(at, n=128):
            return cst[:, at:at + n]

        def V(name):
            a, b = V_LAY[name]
            return vec[:, a:b]

        ident, ones = C(C_ID), C(C_ONE)
        eps = cst[:, C_EPS:C_EPS + 1]

        mhalf = cst[:, C_MHALF:C_MHALF + 2]

        def stat(n, k, width=1):
            return st[:, 64 + 16 * n + k:64 + 16 * n + k + width]

        def norm_scale(n, tt):
            return stat(n, 10 + 2 * tt + (n == 2))

        S = {}

        def s(name):
            if name not in S:
                S[name] = sem(name)
            return S[name]

        raw_full = [sem(f"raw_full{i}") for i in range(RAW)]
        hi_made = sem("hi_made")
        lo_made = sem("lo_made")
        slab_used = sem("slab_used")

        class Chain:

            def __init__(self, name):
                self.sem, self.n, self.i, self.per = sem(name), 0, None, 0

            def value(self):
                return self.n if self.i is None else self.n + self.i * self.per

            def step(self, eng, ins):
                ins.then_inc(self.sem, 1)
                self.n += 1
                eng.wait_ge(self.sem, self.value())

            def mark(self, ins):
                ins.then_inc(self.sem, 1)
                self.n += 1
                return self.value()

            def loop(self, i, per):
                self.i, self.per, self.start = i, per, self.n

            def end(self, times):
                assert self.n - self.start == self.per, (self.n - self.start, self.per)
                self.n, self.i = self.start + self.per * times, None

        tenants = [[] for _ in range(8)]
        lease = {}
        bank_full = [sem(f"bank_full{b}") for b in range(8)]
        bank_free = [sem(f"bank_free{b}") for b in range(8)]

        def tenant(name, bank, gives_back=1):
            filled, freed = sum(n > 0 for n in tenants[bank]), sum(tenants[bank])
            tenants[bank].append(gives_back)
            lease[name] = (bank, filled + 1, freed, gives_back)

        def bank(name):
            return ps[:, lease[name][0], :]

        def full(name):
            return bank_full[lease[name][0]], lease[name][1]

        def fills(name):
            return bank_full[lease[name][0]], 1

        def frees(name):
            return bank_free[lease[name][0]], 1

        def given_back(name):
            b, _, before, gives_back = lease[name]
            return bank_free[b], before + gives_back

        def take_bank(pe, name):
            b, _, n, _ = lease[name]
            if n:
                pe.wait_ge(bank_free[b], n)

        for q in range(4):
            tenant(f"n0_{q}", 4 + q, 2)
        tenant("gg", 3)
        tenant("z", 2, 2)
        for i, n in enumerate(IN1):
            tenant(n, i % 2)
        for n in ("mq0", "mk0", "mq1", "mk1"):
            tenant(n + "r", 2)
        for L in GLA_LEVELS:
            for par in range(2):
                tenant(f"lev{L}_{par}", 3 + par)
        tenant("go0", 4)
        tenant("go1", 3)
        for j in range(2):
            tenant(f"gs{j}", 4 - j)
        for hh in range(MOBA_H):
            tenant(f"ms{hh}", 5)
            tenant(f"mt{hh}", 6)
            if hh % 2 == 0:
                tenant(f"mo{hh // 2}", 7)
        for q in range(4):
            tenant(f"w1_{q}", q, 0)
        for q in range(4):
            tenant(f"n1_{q}", 4 + q, 2)
        FREE = {"ffn1": 2, "ffn2": 1}
        ffn_lease = {}

        def ffn_tenants(k):
            for q in range(4):
                tenant(f"{k}_acc{q}", q, 0)
            ffn_lease[k] = [(len(tenants[4 + b]), sum(tenants[4 + b])) for b in range(4)]
            for f in range(FF):
                for j in range(2):
                    tenants[4 + 2 * (f % 2) + j].append(FREE[k])

        ffn_tenants("ffn1")
        for q in range(4):
            tenant(f"n2_{q}", 4 + q, 2)
        for n, b in (("sq", 0), ("sk", 1), ("sv", 0), ("fq", 6), ("fk", 7), ("fv", 1), ("cc", 0), ("cx", 1), ("cb", 0),
                     ("u", 1), ("v", 0)):
            tenant(n, b, 2 if n in ("fq", "fk") else 1)
        for i, n in enumerate(EARLY):
            tenant(n, (i + 1) % 2)
        for hh in range(4):
            tenant(f"ss{hh}", 2 + hh % 2)
            tenant(f"sr{hh}", 5)
            if hh % 2 == 0:
                tenant(f"so{hh // 2}", 4)
        tenant("fqs", 2)
        tenant("fks", 3)
        tenant("f", 5)
        for hh in range(FOX_H):
            tenant(f"fs{hh}", 2 + hh % 2)
            tenant(f"ft{hh}", 5)
            if hh % 2 == 0:
                tenant(f"fo{hh // 2}", 7)
        tenant("gm", 6)
        for m in range(4):
            tenant(f"l2_{m}", 4)
            tenant(f"l3_{m}", 5)
            for n in range(N_BRANCH):
                tenant(f"br{m}_{n}", (6, 7, 4, 5)[n])
        for q in range(4):
            tenant(f"w2_{q}", q, 0)
        for q in range(4):
            tenant(f"n3_{q}", 4 + q, 2)
        ffn_tenants("ffn2")

        def hidden(k, f, j):
            return ps[:, 4 + 2 * (f % 2) + j, :]

        def hidden_full(k, f, j, i=None):
            b = 2 * (f % 2) + j
            n = ffn_lease[k][b][0] + f // 2 + 1
            return bank_full[4 + b], n if i is None else n + i

        def hidden_free(k, f, j, i=None, done=True):
            b = 2 * (f % 2) + j
            n = ffn_lease[k][b][1] + (f // 2 + done) * FREE[k]
            return bank_free[4 + b], n if i is None else n + i * FREE[k]

        down_used = {"ffn1": sem("down_used1"), "ffn2": sem("down_used2")}
        proj_used = {"out1": sem("proj_used1"), "mix2": sem("proj_used2")}

        def consumed(n, i=None):
            stage, name = STREAM[n]
            if stage in FREE:
                f = int(name[1:])
                if name[0] == "d":
                    return down_used[stage], f + 1 if i is None else f + 1 + 2 * i
                return hidden_full(stage, f, "gv".index(name[0]), i)
            if stage == "out1":
                return proj_used[stage], OUT1.index(name) + 1
            if stage == "mix2" and name[0] == "o":
                return proj_used[stage], int(name[1:]) + 1
            if stage == "mix2" and name[0] == "m":
                return full(f"br{name[1:]}_3")
            return full(name)

        def piece(at, *shape):
            n = int(np.prod(shape))
            assert at + n <= arena_w, (at, shape)
            v = arena[:, at:at + n]
            if len(shape) == 1:
                return v
            names = "abcd"[:len(shape)]
            return v.rearrange(f"p ({' '.join(names)}) -> p {' '.join(names)}", **dict(zip(names, shape)))

        xs = piece(0, TT, D)
        junk, junk_act, junk_dve = piece(2048, D), piece(3072, D // 2), piece(3584, D // 2)
        Dl = [piece(512 * j, 2, T) for j in range(2)]
        Kl = [piece(1024 + 512 * j, 2, T) for j in range(2)]
        zb, za, ze = (piece(3072 + 512 * j, 2, T) for j in range(3))
        tmpm = [piece(3072, 4, P), piece(4608, 4, P)]
        ggT = piece(5120, 256)
        gqT, gkT, G = (piece(5376 + 512 * j, 2, T) for j in range(3))
        gv = piece(6912, TT, 2, 256)
        grT = piece(7936, GLA_H, T)
        Acat = piece(8960, GLA_H, 3, P)
        qpre, mrot = [piece(10496, 2, T), piece(14592, 2, T)], piece(11008, 2, T)
        qT, kT = piece(11520, 4, T), piece(12544, 4, T)
        mv = piece(13568, TT, 2, 256)
        osq = [piece(512 * j, 2, T) for j in range(2)]
        og = [piece(1024 + 512 * j, 2, T) for j in range(2)]
        orr = [G, gqT]
        pex1 = [piece(2048 + 384 * j, 384) for j in range(2)]
        pt1 = [piece(3584 + 384 * j, 384) for j in range(2)]
        yb = [piece(4096 + 1024 * j, 4, T) for j in range(2)]
        sil = [piece(6144 + 512 * j, 512) for j in range(2)]
        gt = [piece(7168 + 512 * j, 512) for j in range(2)]
        sg = piece(0, 2, KT, T)
        cc, xc, yv = (piece(4096 + 512 * j, 2, T) for j in range(3))
        zs, ea, Lt, wt = ([piece(at + 384 * j, 384) for j in range(2)] for at in (0, 768, 1536, 2304))
        fsq = [piece(3072 + 512 * j, 2, T) for j in range(2)]
        sgl = [piece(4096 + 1024 * j, 2, 512) for j in range(2)]
        sqT, skT = piece(7168, 2, T), piece(7680, 2, T)
        sv = piece(8192, TT, 256)
        fqp, fkp = piece(5632, FOX_H, T), piece(9216, FOX_H, T)
        fv = piece(10240, TT, 256)
        fz = piece(10752, T)
        uT, vt = piece(11264, 2, T), piece(11776, TT, 256)
        vn = piece(12288, TT, 256)
        frs = [piece(12800, 2, T), piece(13312, 2, T)]
        lsa, lse = piece(13824, T), piece(14080, T)
        pex2 = [piece(12800 + 384 * j, 384) for j in range(2)]
        pt2 = [piece(13568 + 384 * j, 384) for j in range(2)]
        macc = [piece(6144 + 512 * j, 512) for j in range(2)]
        mtmp = [piece(12800 + 512 * j, 512) for j in range(2)]
        onesT = piece(14336, T)
        mh_all, ml_all = (t[:, :, :].rearrange("p k c -> p (k c)")[:, 0:1024].rearrange("p (a b) -> p a b", a=4)
                          for t in (smh, sml))

        def merged(t, m):
            return t[:, :, :].rearrange("p k c -> p (k c)")[:, 512 * (m % 2):512 * (m % 2) + 512]

        levels_after = {k: [L for L in GLA_LEVELS if LEVEL_SLAB[L] == k] for k in range(2, 10)}

        def small_parts(dst):
            small = V("small").rearrange("p (k c) -> p k c", k=KT)
            return [(dst[:, :, 0:GATE_RANK], small[:, :, 0:GATE_RANK]),
                    (dst[:, :, GATE_RANK:].rearrange("p k (a b) -> p k a b", a=4)[:, :, :, 0:2],
                     small[:, :, GATE_RANK:].rearrange("p k (a b) -> p k a b", a=4))]

        def pv_signal(hh):
            name = f"mo{hh // 2}" if hh < 8 else f"fo{(hh - 8) // 2}"
            return fills(name) if hh % 2 else (s("pv_first"), 1)

        def pv_done(hh):
            name = f"mo{hh // 2}" if hh < 8 else f"fo{(hh - 8) // 2}"
            return full(name) if hh % 2 else (s("pv_first"), hh // 2 + 1)

        def stick_signal(i):
            return fills(f"so{i // 2}") if i % 2 else (s("stick_first"), 1)

        def stick_done(i):
            return full(f"so{i // 2}") if i % 2 else (s("stick_first"), i // 2 + 1)

        def halves(ap):
            return ap.rearrange("p (a b) -> p a b", b=128)[:, 0:3:2, :]

        block = ctx.enter_context(nc.Block())

        @block.sync
        def _(sp):
            for tt in range(TT):
                sp.dma_start(h[:, tt, :], x_in[tt * P:(tt + 1) * P, :]).then_inc(s(f"x{tt}_in"), 16)
                if tt == 0:
                    sp.dma_start(cst[:, 0:C_FIRST], cst_in[:, 0:C_FIRST]).then_inc(s("cst_first_in"), 16)
            sp.dma_start(vec[:, 0:V_FIRST], vec_in[:, 0:V_FIRST]).then_inc(s("vec_first_in"), 16)
            sp.dma_start(raw[:, 0, :], slabs_in[0]).then_inc(raw_full[0], 16)
            for j in range(1, RAW):
                sp.dma_start(raw[:, j, :], slabs_in[j]).then_inc(raw_full[j], 16)
            sp.dma_start(cst[:, C_FIRST:], cst_in[:, C_FIRST:]).then_inc(s("cst_rest_in"), 16)
            for n in range(RAW, 2 * RAW):
                sp.wait_ge(lo_made, n - RAW + 1)
                sp.dma_start(raw[:, n % RAW, :], slabs_in[n]).then_inc(raw_full[n % RAW], 16)
            sp.dma_start(vec[:, V_FIRST:], vec_in[:, V_FIRST:]).then_inc(s("vec_rest_in"), 16)
            with sp.Fori(2, NS // RAW) as i:
                for j in range(RAW):
                    sp.wait_ge(lo_made, i * RAW + (j + 1 - RAW))
                    sp.dma_start(raw[:, j, :], slabs_in[i * RAW + j]).then_inc(raw_full[j], 16)
            for n in range(NS // RAW * RAW, NS):
                sp.wait_ge(lo_made, n - RAW + 1)
                sp.dma_start(raw[:, n % RAW, :], slabs_in[n]).then_inc(raw_full[n % RAW], 16)
            for tt in range(TT):
                sp.wait_ge(s("h_made"), 12 + 2 * (tt + 1))
                sp.dma_start(out[tt * P:(tt + 1) * P, :], h[:, tt, :]).then_inc(s("out_sent"), 16)
            sp.wait_ge(s("out_sent"), 16 * TT)

        @block.gpsimd
        def _(pool):
            me = Chain("pool_step")

            def inverse_roots(n, tt):
                pool.wait_ge(s(f"ssq{tt}_made"), (n + 1) * (1 + tt))
                mean = stat(n, 6 + 2 * tt)
                if tt == 0:
                    me.step(pool, pool.tensor_scalar(mean, stat(n, 0), EPS, None, ALU.add))
                else:
                    me.step(pool, pool.tensor_tensor(mean, stat(n, 1), stat(n, 2), ALU.add))
                wide = 1
                if n == 2:
                    wide = 2
                    me.step(pool, pool.tensor_scalar(stat(n, 7 + 2 * tt), mean, EPS, None, ALU.mult))
                    me.step(pool, pool.tensor_tensor(stat(n, 7 + 2 * tt), stat(n, 7 + 2 * tt), stat(n, 3 + tt), ALU.add))
                pool.tensor_tensor(stat(n, 10 + 2 * tt, wide), stat(n, 6 + 2 * tt, wide), mhalf[:, 0:wide],
                                   ALU.pow).then_inc(s("rstd_made"), 1)

            def scale_level(i):
                pool.wait_ge(s("decay"), i + 1)
                pool.tensor_tensor(Kl[i % 2], Dl[i % 2], gkT, ALU.mult)
                pool.tensor_tensor(Dl[i % 2], Dl[i % 2], gqT, ALU.mult).then_inc(s("level_scaled"), 1)

            pool.memset(zeros[:, :], 0.0).then_inc(s("zeros_made"), 1)
            pool.memset(smh[:, :, :].bitcast(F32), 0.0).then_inc(s("small_zero"), 1)
            pool.memset(sml[:, :, :].bitcast(F32), 0.0).then_inc(s("small_zero"), 1)
            pool.wait_ge(s("cst_first_in"), 16)
            for tt in range(TT):
                inverse_roots(0, tt)
            pool.wait_ge(*given_back("gk"))
            pool.wait_ge(s("gates_summed"), 1)
            for i, L in enumerate(GLA_LEVELS[1:]):
                if i >= 2:
                    pool.wait_ge(*full(f"lev{GLA_LEVELS[i - 1]}_1"))
                nb = 2 * T // (2 * L)
                g = G.rearrange("p a b -> p (a b)").rearrange("p (n l) -> p n l", n=nb)
                d = Dl[i % 2].rearrange("p a b -> p (a b)").rearrange("p (n l) -> p n l", n=nb)
                mid = g[:, :, L - 1:L].broadcast_to([P, nb, L])
                pool.tensor_tensor(d[:, :, L:2 * L], g[:, :, L:2 * L], mid, ALU.subtract)
                pool.tensor_tensor(d[:, :, 0:L], mid, g[:, :, 0:L], ALU.subtract).then_inc(s("level_diff"), 1)
                if i:
                    scale_level(i - 1)
            scale_level(len(GLA_LEVELS) - 2)
            for n in (1, 2):
                for tt in range(TT):
                    inverse_roots(n, tt)
            for j, dst in enumerate((fqp, fkp)):
                pool.tensor_copy(dst, C(C_SEL + 4 * j, 4).unsqueeze(2).broadcast_to([P, FOX_H, T]))\
                    .then_inc(s("fox_filled"), 1)
            pool.wait_ge(s("v_var"), 1)
            me.step(pool, pool.tensor_scalar(st[:, 46:48], st[:, 44:46], EPS, None, ALU.add))
            pool.tensor_tensor(st[:, 30:32], st[:, 46:48], mhalf, ALU.pow).then_inc(s("v_rstd"), 1)
            for tt in range(TT):
                inverse_roots(3, tt)

        @block.scalar
        def _(act):
            me = Chain("act_step")

            def rnd(n, i=None):
                act.wait_ge(raw_full[n % RAW], 16 * (n // RAW + 1) if i is None else 16 * (n // RAW + 1) + i * 32)
                if n >= SPLIT:
                    act.wait_ge(*consumed(n - SPLIT, i))
                act.activation(hiw[:, n % SPLIT, :], raw[:, n % RAW, :], ACT.Copy).then_inc(hi_made, 1)

            def tables(name):
                nc.scalar.preload_act_table_set(name)

            def norm_stats(n):
                act.wait_ge(*((s("h_made"), 4 * n - 2) if n else (s("x0_in"), 16)))
                def squares(dst, src, k):
                    return act.activation(dst, src, ACT.Square, scale=D ** -0.5, accum_out=stat(n, k))

                ins = squares(junk, h[:, 0, :], 0)
                if n == 2:
                    me.step(act, ins)
                    act.wait_ge(s("weighted"), 1)
                    ins = squares(junk, xs[:, 0, :], 3)
                ins.then_inc(s("ssq0_made"), 1)
                act.wait_ge(*((s("h_made"), 4 * n - 1) if n else (s("x1_in"), 16)))
                ins = squares(junk_act, h[:, 1, 0:D // 2], 1)
                if n == 2:
                    act.wait_ge(s("ssq0_made"), n + 1)
                    act.wait_ge(s("weighted"), 2)
                    ins = squares(junk, xs[:, 1, :], 4)
                ins.then_inc(s("ssq1_made"), 1)

            def norm_turned(n):
                for kt in range(KT):
                    act.wait_ge(*full(f"n{n}_{kt // 2}"))
                    act.activation(xhi[:, kt, :], bank(f"n{n}_{kt // 2}")[:, kt % 2 * T:(kt % 2 + 1) * T], ACT.Copy,
                                   scale=V(f"ng{n}")[:, kt:kt + 1]).then_inc(s("xhi_made"), 1)

            def evacuate(name, dst, func=ACT.Copy, scale=1.0):
                act.wait_ge(*full(name))
                src = bank(name)
                if len(dst.shape) == 3:
                    src = src.rearrange("p (a b) -> p a b", a=dst.shape[1])
                return act.activation(dst, src, func, scale=scale).then_inc(*frees(name))

            tables("natural_log_exp_and_others")
            norm_stats(0)
            act.wait_ge(s("cst_first_in"), 16)
            act.wait_ge(s("vec_first_in"), 16)
            act.wait_ge(s("small_zero"), 2)
            for dst, src in small_parts(smh):
                act.activation(dst, src, ACT.Copy).then_inc(s("small_hi"), 1)
            norm_turned(0)
            rnd(0)
            rnd(1)
            rnd(2)
            act.wait_ge(*full("gg"))
            act.activation(ggT[0:GATE_RANK, :], bank("gg")[0:GATE_RANK, 0:T], ACT.Copy).then_inc(*frees("gg"))
            evacuate("gq", gqT, scale=SCALE)
            act.wait_ge(*full("z"))
            for c in range(2):
                act.activation(zb[:, c, :], bank("z")[:, c * T:(c + 1) * T], ACT.Identity,
                               bias=V("bgate")[:, c:c + 1]).then_inc(*frees("z"))
            act.wait_ge(*given_back("z"))
            me.step(act, act.activation(za, zb, ACT.Abs))
            me.step(act, act.activation(ze, za, ACT.Exp, scale=-1.0))
            act.activation(za, ze, ACT.Ln, bias=1.0).then_inc(s("z_ln"), 1)
            rnd(3)
            evacuate("gk", gkT)
            rnd(4)

            def decay(i):
                act.wait_ge(s("level_diff"), i + 1)
                act.activation(Dl[i % 2], Dl[i % 2], ACT.Exp, scale=1.0 / GATE_TAU).then_inc(s("decay"), 1)

            def diag01():
                for par in range(2):
                    act.wait_ge(*full(f"lev128_{par}"))
                    act.activation(Acat[:, par::2, 1, :], bank(f"lev128_{par}")[:, 0:256].rearrange(
                        "p (a b) -> p a b", a=2), ACT.Copy).then_inc(*frees(f"lev128_{par}"))

            def softmax_head(hh, pre, pex):
                act.wait_ge(s("max_made"), hh + 1)
                c = 48 + 8 * (hh % 2)
                if hh >= 2:
                    act.wait_ge(*full(turned_name(hh - 2)))
                act.activation(pex[hh % 2][:, 0:128], bank(f"{pre}{hh % 8}")[:, 0:128], ACT.Exp, scale=SCALE,
                               bias=st[:, c:c + 1], accum_out=st[:, c + 2:c + 3]).then_inc(s("exp_made"), 1)
                act.activation(pex[hh % 2][:, 128:384], bank(f"{pre}{hh % 8}")[:, 128:384], ACT.Exp, scale=SCALE,
                               bias=st[:, c + 1:c + 2], accum_out=st[:, c + 3:c + 4])\
                   .then_inc(*frees(f"{pre}{hh % 8}"))

            def turned_name(hh):
                return f"mt{hh}" if hh < 8 else f"ft{hh - 8}"

            def turned_probs(hh, pt):
                name = turned_name(hh)
                act.wait_ge(*full(name))
                if hh % 8 >= 2:
                    act.wait_ge(*pv_done(hh - 2))
                act.activation(pt[hh % 2], bank(name)[:, 0:384], ACT.Copy).then_inc(*frees(name))

            def head_out(name, chunk):
                act.wait_ge(*full(name))
                act.activation(yhi[:, chunk, :], bank(name)[:, 0:T], ACT.Copy).then_inc(s("head_hi"), 1)

            def gla_norm(j):
                act.wait_ge(*full(f"gs{j}"))
                act.activation(orr[j], bank(f"gs{j}").rearrange("p (a b) -> p a b", a=2), ACT.Ln,
                               scale=1.0 / GLA_V, bias=eps).then_inc(*frees(f"gs{j}"))
                act.wait_ge(*given_back(f"gs{j}"))
                act.activation(orr[j], orr[j], ACT.Exp, scale=-0.5).then_inc(s("o_rstd"), 1)

            def gla_hi(j):
                act.wait_ge(s("gy_made"), j + 1)
                act.activation(yhi[:, 4 + 2 * j:6 + 2 * j, :], orr[j], ACT.Copy).then_inc(s("gy_hi"), 1)

            DST = {"mq0": qpre[0], "mk0": qpre[1], "mq1": qpre[0], "mk1": qpre[1], "mv0": mv[:, :, 0, :],
                   "mv1": mv[:, :, 1, :], "gv0": gv[:, :, 0, :], "gv1": gv[:, :, 1, :], "gr0": grT[:, 0:2, :],
                   "gr1": grT[:, 2:4, :]}
            ropes = 0
            decay(0)
            decay(1)
            for k in range(2, 12):
                name = IN1[k]
                if name in ROPED:
                    if ropes >= 2:
                        act.wait_ge(s("roped"), ropes - 1)
                    ropes += 1
                evacuate(name, DST[name])
                if k == 10:
                    for j in range(2):
                        act.wait_ge(*full(f"go{j}"))
                        act.activation(osq[j], bank(f"go{j}").rearrange("p (a b) -> p a b", a=2),
                                       ACT.Square).then_inc(s("o_sq"), 1)
                        evacuate(f"go{j}", og[j])
                if k < 11:
                    rnd(k + 3)
                if k == 2:
                    diag01()
                if 2 <= k <= 7:
                    decay(k)
                if k == 11:
                    for j in range(2):
                        gla_norm(j)
                if k >= 6:
                    turned_probs(k - 6, pt1)
                if k >= 5:
                    softmax_head(k - 5, "ms", pex1)
                if k in (8, 10):
                    head_out(f"mo{(k - 8) // 2}", (k - 8) // 2)
            act.wait_ge(*given_back("gr1"))
            tables("silu_and_others")
            act.activation(grT, grT, ACT.Silu).then_inc(s("silu_gates"), 1)
            tables("natural_log_exp_and_others")
            for j in range(2):
                gla_hi(j)
            rnd(14)
            softmax_head(7, "ms", pex1)
            turned_probs(6, pt1)
            rnd(15)
            head_out("mo2", 2)
            turned_probs(7, pt1)
            rnd(16)
            head_out("mo3", 3)
            first_ffn = AT[("ffn1", "g0")]
            rnd(first_ffn + 1)
            norm_stats(1)
            act.wait_ge(s("vec_rest_in"), 16)
            norm_turned(1)
            rnd(first_ffn + 2)

            def ffn_step(k, f, i=None):
                b = AT[(k, "g0")]
                splits = [b + 3] if f == 0 else [b + 4 + 3 * (f - 1) + j for j in range(3)]
                splits = [n for n in splits if n < NS]
                splits, later = (splits[:1], splits[1:]) if f == FF - 1 else (splits, [])
                par = f % 2
                for j in range(2):
                    for n in splits[j:j + 1] + (splits[2:] if j else []):
                        rnd(n, i)
                    act.wait_ge(*hidden_full(k, f, j, i))
                    if k == "ffn1":
                        for c in range(2):
                            ch = j * (NCH // 2) + 2 * f + c
                            if i is None:
                                sc, bi = V("cw")[:, 2 * NCH + ch:2 * NCH + ch + 1], V("cb")[:, ch:ch + 1]
                            else:
                                sc = vec[:, bass.ds(V_LAY["cw"][0] + 2 * NCH + ch + 4 * i, 1)]
                                bi = vec[:, bass.ds(V_LAY["cb"][0] + ch + 4 * i, 1)]
                            act.activation(yb[par][:, 2 * j + c, :], hidden(k, f, j)[:, c * T:(c + 1) * T],
                                           ACT.Identity, scale=sc, bias=bi).then_inc(s("tap2"), 1)
                    elif j == 0:
                        act.activation(sil[par], hidden(k, f, 0), ACT.Silu).then_inc(hidden_free(k, f, 0)[0], 1)
                if k == "ffn1":
                    act.wait_ge(*hidden_free(k, f, 0, i))
                    act.activation(sil[par], yb[par][:, 0:2, :].rearrange("p a b -> p (a b)"),
                                   ACT.Silu).then_inc(s("silu_made"), 1)
                    act.wait_ge(s("gated"), f + 1 if i is None else f + 1 + 2 * i)
                else:
                    act.wait_ge(*hidden_free(k, f, 1, i))
                if f >= 2:
                    act.wait_ge(down_used[k], f - 1 if i is None else f - 1 + 2 * i)
                act.activation(yhi[:, 2 * par:2 * par + 2, :].rearrange("p a b -> p (a b)"), gt[par],
                               ACT.Copy).then_inc(s(f"g_hi_{k}"), 1)
                for n in later:
                    rnd(n)

            def ffn(k):
                ffn_step(k, 0)
                ffn_step(k, 1)
                with act.Fori(0, FFN_PAIRS) as i:
                    ffn_step(k, 2, i)
                    ffn_step(k, 3, i)
                for f in range(FF - 3, FF):
                    ffn_step(k, f)

            ffn("ffn1")
            b2 = AT[("in2", IN2[0])]
            rnd(b2 + 1)
            norm_stats(2)
            norm_turned(2)
            rnd(b2 + 2)

            def y_hi(k, chunk, src, wait):
                act.wait_ge(*wait)
                act.activation(yhi[:, chunk:chunk + 2, :], src, ACT.Copy).then_inc(s(f"y_hi{k}"), 1)

            def stick_a(i):
                if i >= 2:
                    act.wait_ge(*stick_done(i - 2))
                act.wait_ge(*given_back(f"ss{i}"))
                me.step(act, act.activation(ea[i % 2], zs[i % 2], ACT.Abs))
                me.step(act, act.activation(wt[i % 2], ea[i % 2], ACT.Exp, scale=-1.0))
                act.activation(ea[i % 2], wt[i % 2], ACT.Ln, bias=1.0).then_inc(s("stick_ln"), 1)

            def stick_b(i):
                act.wait_ge(*given_back(f"sr{i}"))
                act.activation(wt[i % 2], zs[i % 2], ACT.Exp).then_inc(s("stick_w"), 1)

            def fox_square(j):
                act.wait_ge(*full(("fq", "fk")[j]))
                act.activation(fsq[j], bank(("fq", "fk")[j]).rearrange("p (a b) -> p a b", a=2),
                               ACT.Square).then_inc(s("f_sq"), 1)

            def fox_norms():
                for j, n in enumerate(("fqs", "fks")):
                    act.wait_ge(*full(n))
                    act.activation(frs[j], bank(n).rearrange("p (a b) -> p a b", a=2), ACT.Ln,
                                   scale=1.0 / HD, bias=eps).then_inc(*frees(n))
                    act.wait_ge(*given_back(n))
                    act.activation(frs[j], frs[j], ACT.Exp, scale=-0.5).then_inc(s("f_rstd"), 1)

            def forget_gates():
                act.wait_ge(*full("f"))
                act.activation(fz, bank("f")[:, 0:T], ACT.Identity, bias=V("bf")).then_inc(*frees("f"))
                act.wait_ge(*given_back("f"))
                me.step(act, act.activation(lsa, fz, ACT.Abs))
                me.step(act, act.activation(lse, lsa, ACT.Exp, scale=-1.0))
                act.activation(lsa, lse, ACT.Ln, bias=1.0).then_inc(s("f_ln"), 1)

            def early_gate(i):
                n = EARLY[i]
                br, m = int(n[1]), int(n[3])
                evacuate(n, sg[:, br, 2 * m:2 * m + 2, :])

            tables("natural_log_exp_and_others")
            for k in range(19):
                if k >= 11:
                    early_gate(k - 11)
                elif IN2[k] in ("sq", "sk", "sv", "fv", "cc", "u", "v"):
                    evacuate(IN2[k], {"sq": sqT, "sk": skT, "sv": sv, "fv": fv, "cc": cc, "u": uT, "v": vt}[IN2[k]])
                if k in (3, 4):
                    fox_square(k - 3)
                if 3 <= k <= 6:
                    stick_b(k - 3)
                rnd(b2 + k + 3)
                if k == 6:
                    fox_norms()
                if 2 <= k <= 5:
                    stick_a(k - 2)
                if k in (5, 7):
                    head_out(f"so{(k - 5) // 2}", 4 + (k - 5) // 2)
                if k == 7:
                    act.wait_ge(*given_back("cx"))
                    for c in range(2):
                        act.activation(yv[:, c, :], xc[:, c, :], ACT.Copy,
                                       scale=V("wc2")[:, 4 + c:5 + c]).then_inc(s("yv_tap"), 1)
                    forget_gates()
                if k == 8:
                    y_hi("a", 0, yv, given_back("cb"))
                if 10 <= k <= 13:
                    turned_probs(8 + k - 10, pt2)
                if 9 <= k <= 12:
                    softmax_head(8 + k - 9, "fs", pex2)
                if k in (12, 14):
                    head_out(f"fo{(k - 12) // 2}", 6 + (k - 12) // 2)
                if k == 14:
                    act.wait_ge(*given_back("v"))
                    act.activation(uT, uT, ACT.Gelu_apprx_tanh)
                    for tt in range(TT):
                        act.activation(vt[:, tt, :], vt[:, tt, :], ACT.Gelu_apprx_tanh,
                                       accum_out=st[:, 42 + tt:43 + tt]).then_inc(s("v_gelu"), 1)
            y_hi("b", 2, vt, (s("yb_made"), 1))

            base = AT[("mix2", "l2_0")]
            nxt = [base + 3]
            def rnd_to(n):
                while nxt[0] <= n and nxt[0] < NS:
                    rnd(nxt[0])
                    nxt[0] += 1
            nxt[0] = b2 + 22
            assert b2 + 22 == base + 3
            for m in range(4):
                act.activation(sg[:, :, 2 * m:2 * m + 2, :], sg[:, :, 2 * m:2 * m + 2, :],
                               ACT.Sigmoid).then_inc(s("early_gates"), 1)
                if m >= 2:
                    act.wait_ge(s("merged"), m - 1)
                for j in range(2):
                    evacuate(f"l{2 + j}_{m}", sgl[m % 2][:, j, :], ACT.Sigmoid)
                    rnd_to(AT[("mix2", f"l{2 + j}_{m}")] + 3)
                rnd_to(AT[("mix2", f"m{m}")] + 3)
                act.wait_ge(s("merged"), m + 1)
                if m >= 2:
                    act.wait_ge(proj_used["mix2"], m - 1)
                act.activation(merged(smh, m), macc[m % 2], ACT.Copy).then_inc(s("merged_hi"), 1)
                if m:
                    rnd_to(AT[("mix2", f"o{m - 1}")] + 3)
            rnd_to(AT[("ffn2", "g0")] + 1)
            norm_stats(3)
            norm_turned(3)
            rnd_to(AT[("ffn2", "g0")] + 2)
            ffn("ffn2")

        @block.vector
        def _(dve):
            me = Chain("dve_step")

            def res(n, i=None):
                dve.wait_ge(hi_made, n + 1 if i is None else n + 1 + 6 * i)
                dve.tensor_tensor(low[:, n % SPLIT, :], raw[:, n % RAW, :], hiw[:, n % SPLIT, :].bitcast(F32),
                                  ALU.subtract).then_inc(lo_made, 1)

            def norm_tile1(n):
                dve.wait_ge(*((s("h_made"), 4 * n) if n else (s("x1_in"), 16)))
                half = h[:, 1, D // 2:]
                dve.tensor_tensor_reduce(junk_dve, half, half, 1.0 / D, EPS, ALU.mult, ALU.add,
                                         stat(n, 2)).then_inc(s("ssq1_made"), 1)

            def norm_diagonal(n, tt):
                dve.wait_ge(s("rstd_made"), 2 * n + tt + 1)
                dve.tensor_scalar(diag[:, tt, :], ident, norm_scale(n, tt), None, ALU.mult).then_inc(s("diag_made"), 1)

            def weighted(tt):
                dve.wait_ge(s("h_made"), 4 + 2 * (tt + 1))
                dve.tensor_tensor(xs[:, tt, :], h[:, tt, :], V("fg"), ALU.mult).then_inc(s("weighted"), 1)

            def norm(n, used, split=None):
                for tt in range(TT):
                    if tt == 0:
                        dve.wait_ge(s("first_tile_out"), n)
                    else:
                        dve.wait_ge(*used)
                    for nh in range(2):
                        dst = h[:, tt, nh * 512:(nh + 1) * 512]
                        dve.tensor_tensor(dst, ps[:, 2 * tt + nh, :], dst, ALU.add).then_inc(s("h_made"), 1)
                    if n == 2:
                        weighted(tt)
                    if tt == 0 and split is not None:
                        res(split)
                if n == 4:
                    return
                norm_tile1(n)
                for tt in range(TT):
                    norm_diagonal(n, tt)
                norm_turned(n)

            def norm_turned(n):
                for kt in range(KT):
                    dve.wait_ge(s("xhi_made"), KT * n + (kt | 1) + 1)
                    dve.scalar_tensor_tensor(
                        out=xlo[:, kt, :], in0=bank(f"n{n}_{kt // 2}")[:, kt % 2 * T:(kt % 2 + 1) * T],
                        scalar=V(f"ng{n}")[:, kt:kt + 1], in1=xhi[:, kt, :].bitcast(F32), op0=ALU.mult,
                        op1=ALU.subtract).then_inc(*frees(f"n{n}_{kt // 2}"))

            def two(name):
                return bank(name).rearrange("p (a b) -> p a b", a=2)

            norm_tile1(0)
            dve.wait_ge(s("cst_first_in"), 16)
            for tt in range(TT):
                norm_diagonal(0, tt)
            dve.wait_ge(s("small_hi"), 2)
            for (dst, src), (hi, _) in zip(small_parts(sml), small_parts(smh)):
                dve.tensor_tensor(dst, src, hi.bitcast(F32), ALU.subtract).then_inc(s("small_lo"), 1)
            norm_turned(0)
            res(0)
            dve.memset(onesT, 1.0).then_inc(s("ones_made"), 1)
            res(1)
            res(2)
            dve.wait_ge(s("z_ln"), 1)
            dve.wait_ge(s("ones_made"), 1)
            me.step(dve, dve.scalar_tensor_tensor(out=zb, in0=zb, scalar=0.0, in1=za, op0=ALU.min, op1=ALU.subtract))
            for c in range(2):
                last = dve.tensor_tensor_scan(G[:, c, :], onesT, zb[:, c, :], 0.0, ALU.mult, ALU.add)
            last.then_inc(s("gates_summed"), 1)
            res(3)
            dve.wait_ge(s("cst_rest_in"), 16)

            def level_scores(L):
                m = C(C_LEV + 128 * MASKED_LEVELS.index(L)).unsqueeze(1).broadcast_to([P, 4, P])
                for par in range(2):
                    dve.wait_ge(*full(f"lev{L}_{par}"))
                    src = bank(f"lev{L}_{par}").rearrange("p (a b) -> p a b", a=4)
                    if L == 0:
                        for blk in range(2):
                            ins = dve.tensor_tensor(Acat[:, par::2, 2 * blk, :], src[:, blk::2, :], m[:, 0:2, :],
                                                    ALU.mult)
                        ins.then_inc(*frees(f"lev{L}_{par}"))
                    else:
                        tmp = tmpm[par]
                        dve.tensor_tensor(tmp, src, m, ALU.mult).then_inc(*frees(f"lev{L}_{par}"))
                        dve.wait_ge(*given_back(f"lev{L}_{par}"))
                        for blk in range(2):
                            ins = dve.tensor_tensor(Acat[:, par::2, 2 * blk, :], Acat[:, par::2, 2 * blk, :],
                                                    tmp[:, blk::2, :], ALU.add)
                        ins.then_inc(s("scores_added"), 1)
                        dve.wait_ge(s("scores_added"), 2 * (MASKED_LEVELS.index(L) - 1) + par + 1)

            def rope(i, name, dst):
                dve.wait_ge(*given_back(name))
                me.step(dve, dve.tensor_tensor(dst, qpre[i % 2], C(C_COS, T).unsqueeze(1).broadcast_to([P, 2, T]), ALU.mult))
                dve.wait_ge(*full(name + "r"))
                dve.tensor_tensor(mrot, two(name + "r"), C(C_SIN, T).unsqueeze(1).broadcast_to([P, 2, T]),
                                  ALU.mult).then_inc(*frees(name + "r"))
                dve.wait_ge(*given_back(name + "r"))
                dve.tensor_tensor(dst, dst, mrot, ALU.add).then_inc(s("roped"), 1)

            def masked_max(hh, name):
                dve.wait_ge(*full(name))
                me.step(dve, dve.tensor_tensor(halves(bank(name)[:, 0:384]), halves(bank(name)[:, 0:384]),
                                               C(C_NEG).unsqueeze(1).broadcast_to([P, 2, P]), ALU.add))
                c = 48 + 8 * (hh % 2)
                dve.tensor_reduce(st[:, c + 6:c + 7], bank(name)[:, 0:128], AX_X, ALU.max)
                me.step(dve, dve.tensor_reduce(st[:, c + 7:c + 8], bank(name)[:, 128:384], AX_X, ALU.max))
                if hh >= 2:
                    dve.wait_ge(s("probs_made"), hh - 1)
                dve.tensor_scalar(st[:, c:c + 2], st[:, c + 6:c + 8], -SCALE, None, ALU.mult).then_inc(s("max_made"), 1)

            def probs(hh, name, pex):
                c = 48 + 8 * (hh % 2)
                dve.wait_ge(s("exp_made"), hh + 1)
                dve.wait_ge(*given_back(name))
                me.step(dve, dve.reciprocal(st[:, c + 4:c + 6], st[:, c + 2:c + 4]))
                dve.tensor_scalar(pex[hh % 2][:, 0:128], pex[hh % 2][:, 0:128], st[:, c + 4:c + 5], None, ALU.mult)
                dve.tensor_scalar(pex[hh % 2][:, 128:384], pex[hh % 2][:, 128:384], st[:, c + 5:c + 6], None,
                                  ALU.mult).then_inc(s("probs_made"), 1)

            head_outs = [0]

            def head_lo(name, chunk):
                head_outs[0] += 1
                dve.wait_ge(s("head_hi"), head_outs[0])
                dve.tensor_tensor(ylo[:, chunk, :], bank(name)[:, 0:T], yhi[:, chunk, :].bitcast(F32),
                                  ALU.subtract).then_inc(*frees(name))

            def gla_norm(j):
                dve.wait_ge(s("o_rstd"), j + 1)
                me.step(dve, dve.tensor_tensor(orr[j], og[j], orr[j], ALU.mult))
                dve.wait_ge(s("silu_gates"), 1)
                for c in range(2):
                    hh = 2 * j + c
                    ins = dve.scalar_tensor_tensor(out=orr[j][:, c, :], in0=orr[j][:, c, :],
                                                   scalar=V("glag")[:, hh:hh + 1], in1=grT[:, hh, :], op0=ALU.mult,
                                                   op1=ALU.mult)
                ins.then_inc(s("gy_made"), 1)

            def gla_lo(j):
                dve.wait_ge(s("gy_hi"), j + 1)
                dve.tensor_tensor(ylo[:, 4 + 2 * j:6 + 2 * j, :], orr[j], yhi[:, 4 + 2 * j:6 + 2 * j, :].bitcast(F32),
                                  ALU.subtract).then_inc(s("gy_lo"), 1)

            for k in range(1, 12):
                if k == 4:
                    dve.wait_ge(s("vec_rest_in"), 16)
                    dve.tensor_tensor(V("wsp").rearrange("p (a b) -> p a b", a=4), V("wsp").rearrange("p (a b) -> p a b", a=4),
                                      C(C_TRI).unsqueeze(1).broadcast_to([P, 4, P]), ALU.mult).then_inc(s("wsp_masked"), 1)
                if k >= 5:
                    masked_max(k - 5, f"ms{k - 5}")
                for L in levels_after.get(k, []):
                    if L != 128:
                        level_scores(L)
                for i, n in enumerate(ROPED):
                    if IN1.index(n) + 1 == k:
                        rope(i, n, (qT if n[1] == "q" else kT)[:, 2 * int(n[2]):2 * int(n[2]) + 2, :])
                if k < 11:
                    res(k + 3)
                if k in (8, 10):
                    head_lo(f"mo{(k - 8) // 2}", (k - 8) // 2)
                if k >= 5:
                    probs(k - 5, f"ms{k - 5}", pex1)
            for j in range(2):
                gla_norm(j)
            for j in range(2):
                gla_lo(j)
            masked_max(7, "ms7")
            res(14)
            probs(7, "ms7", pex1)
            res(15)
            head_lo("mo2", 2)
            res(16)
            head_lo("mo3", 3)

            first_ffn = AT[("ffn1", "g0")]
            res(first_ffn + 1)
            norm(1, (proj_used["out1"], 4))
            res(first_ffn + 2)

            def ffn_step(k, f, i=None):
                b = AT[(k, "g0")]
                splits = [b + 3] if f == 0 else [b + 4 + 3 * (f - 1) + j for j in range(3)]
                splits = [n for n in splits if n < NS]
                splits, later = (splits[:1], splits[1:]) if f == FF - 1 else (splits, [])
                par = f % 2
                for j in range(2):
                    for n in splits[j:j + 1] + (splits[2:] if j else []):
                        res(n, i)
                    if k == "ffn1":
                        for c in range(2):
                            ch = j * (NCH // 2) + 2 * f + c
                            t = 4 * f + 2 * j + 2
                            dve.wait_ge(s("tap2"), t if i is None else t + 8 * i)
                            dst, src = yb[par][:, 2 * j + c, :], hidden(k, f, j)[:, c * T:(c + 1) * T]
                            for tap in (1, 0):
                                o = 2 - tap
                                if i is None:
                                    w = V("cw")[:, tap * NCH + ch:tap * NCH + ch + 1]
                                else:
                                    w = vec[:, bass.ds(V_LAY["cw"][0] + tap * NCH + ch + 4 * i, 1)]
                                ins = dve.scalar_tensor_tensor(out=dst[:, o:], in0=src[:, 0:T - o], scalar=w,
                                                               in1=dst[:, o:], op0=ALU.mult, op1=ALU.add)
                                if tap:
                                    me.step(dve, ins)
                                else:
                                    ins.then_inc(hidden_free(k, f, j)[0], 1)
                if k == "ffn1":
                    dve.wait_ge(s("silu_made"), f + 1 if i is None else f + 1 + 2 * i)
                    dve.wait_ge(*hidden_free(k, f, 1, i))
                    dve.tensor_tensor(gt[par], sil[par], yb[par][:, 2:4, :].rearrange("p a b -> p (a b)"),
                                      ALU.mult).then_inc(s("gated"), 1)
                else:
                    dve.wait_ge(*hidden_free(k, f, 0, i))
                    dve.wait_ge(*hidden_full(k, f, 1, i))
                    dve.tensor_tensor(gt[par], hidden(k, f, 1), sil[par], ALU.mult).then_inc(hidden_free(k, f, 1)[0], 1)
                dve.wait_ge(s(f"g_hi_{k}"), f + 1 if i is None else f + 1 + 2 * i)
                dve.tensor_tensor(ylo[:, 2 * par:2 * par + 2, :].rearrange("p a b -> p (a b)"), gt[par],
                                  yhi[:, 2 * par:2 * par + 2, :].rearrange("p a b -> p (a b)").bitcast(F32),
                                  ALU.subtract).then_inc(s(f"g_lo_{k}"), 1)
                for n in later:
                    res(n)

            def ffn(k):
                ffn_step(k, 0)
                ffn_step(k, 1)
                with dve.Fori(0, FFN_PAIRS) as i:
                    me.loop(i, 8 if k == "ffn1" else 0)
                    ffn_step(k, 2, i)
                    ffn_step(k, 3, i)
                    me.end(FFN_PAIRS)
                for f in range(FF - 3, FF):
                    ffn_step(k, f)

            ffn("ffn1")
            b2 = AT[("in2", IN2[0])]
            norm(2, (down_used["ffn1"], FF))
            res(b2 + 1)
            for tt in range(TT):
                dve.tensor_scalar(h[:, tt, :], xs[:, tt, :], stat(2, 10 + 2 * tt), None, ALU.mult)
            res(b2 + 2)

            def y_lo(k, chunk, src):
                dve.wait_ge(s(f"y_hi{k}"), 1)
                dve.tensor_tensor(ylo[:, chunk:chunk + 2, :], src, yhi[:, chunk:chunk + 2, :].bitcast(F32),
                                  ALU.subtract).then_inc(s("y_lo"), 1)

            def stick_scores(i):
                dve.wait_ge(*full(f"ss{i}"))
                if i >= 2:
                    dve.wait_ge(s("stick_w"), i - 1)
                z = bank(f"ss{i}")
                dve.scalar_tensor_tensor(out=halves(zs[i % 2]), in0=halves(z[:, 0:384]), scalar=SCALE,
                                         in1=C(C_STN).unsqueeze(1).broadcast_to([P, 2, P]), op0=ALU.mult, op1=ALU.add)
                dve.tensor_scalar(zs[i % 2][:, 128:256], z[:, 128:256], SCALE, None, ALU.mult).then_inc(*frees(f"ss{i}"))

            def stick_soft(i):
                dve.wait_ge(s("stick_ln"), i + 1)
                dve.scalar_tensor_tensor(out=Lt[i % 2], in0=zs[i % 2], scalar=0.0, in1=ea[i % 2], op0=ALU.max,
                                         op1=ALU.add).then_inc(s("stick_soft"), 1)

            def stick_arg(i):
                dve.wait_ge(*full(f"sr{i}"))
                dve.tensor_tensor(zs[i % 2], zs[i % 2], bank(f"sr{i}")[:, 0:384], ALU.subtract)\
                   .then_inc(*frees(f"sr{i}"))

            def fox_normed(j):
                dve.wait_ge(s("f_rstd"), j + 1)
                dve.wait_ge(s("fox_filled"), 2)
                name, dst = ("fq", "fk")[j], (fqp, fkp)[j]
                for par in range(2):
                    r = slice(64 * par, 64 * par + 64)
                    dve.scalar_tensor_tensor(out=dst[r, par::2, :], in0=two(name)[r], scalar=V(name + "g")[r],
                                             in1=frs[j][r], op0=ALU.mult, op1=ALU.mult).then_inc(*frees(name))

            def forget_sums():
                dve.wait_ge(s("f_ln"), 1)
                me.step(dve, dve.scalar_tensor_tensor(out=lse, in0=fz, scalar=0.0, in1=lsa, op0=ALU.min,
                                                      op1=ALU.subtract))
                me.step(dve, dve.tensor_tensor_scan(lsa, onesT, lse, 0.0, ALU.mult, ALU.add))
                for par in range(2):
                    o = 64 * (1 - par)
                    for dst, at, scale in ((fqp, o, 1.0 / SCALE), (fkp, o + 32, -1.0 / SCALE)):
                        ins = dve.tensor_scalar(dst[at:at + 2, par::2, :],
                                                lsa[at:at + 2, :].unsqueeze(1).broadcast_to([2, 2, T]), scale, None,
                                                ALU.mult)
                ins.then_inc(s("forget_made"), 1)

            def conv_taps():
                for c in range(2):
                    dve.wait_ge(s("yv_tap"), c + 1)
                    for tap in (1, 0):
                        o = 2 - tap
                        me.step(dve, dve.scalar_tensor_tensor(
                            out=yv[:, c, o:], in0=xc[:, c, 0:T - o], scalar=V("wc2")[:, 2 * tap + c:2 * tap + c + 1],
                            in1=yv[:, c, o:], op0=ALU.mult, op1=ALU.add))

            def layer_norm_sums():
                dve.wait_ge(s("v_gelu"), 2)
                me.step(dve, dve.tensor_scalar(st[:, 28:30], st[:, 42:44], -1.0 / MIX2, None, ALU.mult))
                for tt in range(TT):
                    ins = dve.tensor_scalar(vn[:, tt, :], vt[:, tt, :], st[:, 28 + tt:29 + tt], None, ALU.add)
                me.step(dve, ins)
                for tt in range(TT):
                    ins = dve.tensor_tensor_reduce(vt[:, tt, :], vn[:, tt, :], vn[:, tt, :], 1.0 / MIX2, 0.0, ALU.mult,
                                                   ALU.add, st[:, 44 + tt:45 + tt])
                ins.then_inc(s("v_var"), 1)

            def layer_norm():
                dve.wait_ge(s("v_rstd"), 1)
                for tt in range(TT):
                    ins = dve.scalar_tensor_tensor(out=vn[:, tt, :], in0=vn[:, tt, :], scalar=st[:, 30 + tt:31 + tt],
                                                   in1=V("lng"), op0=ALU.mult, op1=ALU.mult)
                me.step(dve, ins)
                dve.tensor_tensor(vn, vn, V("lnb").unsqueeze(1).broadcast_to([P, 2, 256]),
                                  ALU.add).then_inc(s("v_normed"), 1)

            def spatial_gate():
                dve.wait_ge(*full("gm"))
                gm = bank("gm").rearrange("p (a c b) -> p a c b", a=2, c=2)
                bsp = V("bsp").rearrange("p (a b) -> p a b", a=2)
                yb4 = vt.rearrange("p a (c b) -> p a c b", c=2)
                for a in range(2):
                    ins = dve.tensor_tensor(yb4[:, a], gm[:, a], bsp[:, a, :].unsqueeze(1).broadcast_to([P, 2, P]),
                                            ALU.add)
                ins.then_inc(*frees("gm"))
                dve.wait_ge(*given_back("gm"))
                dve.tensor_tensor(vt, vt, uT, ALU.mult).then_inc(s("yb_made"), 1)

            dve.memset(onesT, 1.0)
            for k in range(19):
                if 2 <= k <= 5:
                    stick_scores(k - 2)
                if 3 <= k <= 6:
                    stick_arg(k - 3)
                if k == 7:
                    dve.wait_ge(*given_back("cc"))
                    dve.wait_ge(*full("cx"))
                    dve.tensor_tensor(xc, two("cx"), cc, ALU.mult).then_inc(*frees("cx"))
                if k == 8:
                    conv_taps()
                    dve.wait_ge(*full("cb"))
                    dve.tensor_tensor(yv, two("cb"), yv, ALU.mult).then_inc(*frees("cb"))
                    forget_sums()
                if 9 <= k <= 12:
                    masked_max(8 + k - 9, f"fs{k - 9}")
                res(b2 + k + 3)
                if k == 6:
                    for j in range(2):
                        fox_normed(j)
                if 2 <= k <= 5:
                    stick_soft(k - 2)
                if k in (5, 7):
                    head_lo(f"so{(k - 5) // 2}", 4 + (k - 5) // 2)
                if k == 8:
                    y_lo("a", 0, yv)
                if 9 <= k <= 12:
                    probs(8 + k - 9, f"fs{k - 9}", pex2)
                if k in (12, 14):
                    head_lo(f"fo{(k - 12) // 2}", 6 + (k - 12) // 2)
                if k == 15:
                    layer_norm_sums()
                    layer_norm()
                if k == 17:
                    spatial_gate()
            y_lo("b", 2, vt)

            nxt = [b2 + 22]

            def res_to(n):
                while nxt[0] <= n and nxt[0] < NS:
                    res(nxt[0])
                    nxt[0] += 1

            for m in range(4):
                res_to(AT[("mix2", f"l3_{m}")] + 3)
                for n in range(N_BRANCH):
                    if n == N_BRANCH - 1:
                        res_to(AT[("mix2", f"m{m}")] + 2)
                    if n < 2:
                        dve.wait_ge(s("early_gates"), m + 1)
                        gate = sg[:, n, 2 * m:2 * m + 2, :].rearrange("p a b -> p (a b)")
                    else:
                        dve.wait_ge(*given_back(f"l{n}_{m}"))
                        gate = sgl[m % 2][:, n - 2, :]
                    dve.wait_ge(*full(f"br{m}_{n}"))
                    dst = macc[m % 2] if n == 0 else mtmp[n % 2]
                    if m >= 2 and n == 0:
                        dve.wait_ge(s("merged_hi"), m - 1)
                    dve.tensor_tensor(dst, bank(f"br{m}_{n}"), gate, ALU.mult).then_inc(*frees(f"br{m}_{n}"))
                    if n:
                        dve.wait_ge(*given_back(f"br{m}_{n}"))
                        ins = dve.tensor_tensor(macc[m % 2], macc[m % 2], dst, ALU.add)
                        if n < N_BRANCH - 1:
                            me.step(dve, ins)
                        else:
                            ins.then_inc(s("merged"), 1)
                dve.wait_ge(s("merged_hi"), m + 1)
                dve.tensor_tensor(merged(sml, m), macc[m % 2],
                                  merged(smh, m).bitcast(F32), ALU.subtract).then_inc(s("merged_lo"), 1)
                res_to(AT[("mix2", f"m{m}")] + 3)
                if m:
                    res_to(AT[("mix2", f"o{m - 1}")] + (3 if m < 3 else 2))
            norm(3, (proj_used["mix2"], 4), AT[("ffn2", "g0")] + 1)
            nxt[0] += 1
            res_to(AT[("ffn2", "g0")] + 2)
            ffn("ffn2")
            norm(4, (down_used["ffn2"], FF))

        @block.tensor
        def _(pe):
            def keep_clock(name, times):
                for _ in range(times):
                    pe.matmul(bank(name)[:, 0:P], zeros[:, :], zeros[:, :], start=True, stop=True)

            def turn(n):
                src = xs if n == 2 else h
                for q in range(4):
                    take_bank(pe, f"n{n}_{q}")
                keep_clock(f"n{n}_3", WARM[n])
                for tt in range(TT):
                    pe.wait_ge(s("diag_made"), 2 * n + tt + 1)
                    for kt in range(KT):
                        o = bank(f"n{n}_{kt // 2}")[:, kt % 2 * T + tt * P:kt % 2 * T + (tt + 1) * P]
                        mm = pe.matmul(o, src[:, tt, kt * P:(kt + 1) * P], diag[:, tt, :], start=True, stop=True)
                        if tt == TT - 1 and kt % 2:
                            mm.then_inc(*fills(f"n{n}_{kt // 2}"))

            def turned(n, kt):
                if n is not None and kt % 2 == 0:
                    pe.wait_ge(*given_back(f"n{n}_{kt // 2}"))

            def three(o, whi, wlo, mhi, mlo, start, stop):
                pe.matmul(o, whi, mhi, start=start, stop=False)
                pe.matmul(o, whi, mlo, start=False, stop=False)
                return pe.matmul(o, wlo, mhi, start=False, stop=stop)

            def slab_views(n, rows):
                return [t[:, n % SPLIT, :].rearrange("p (k c) -> p k c", k=rows) for t in (hiw, low)]

            def feature_major(o, n, norm=None):
                hi, lo = slab_views(n, KT)
                for c in range(2):
                    for kt in range(KT):
                        turned(norm if c == 0 else None, kt)
                        cc_ = slice(c * P, (c + 1) * P)
                        mm = three(o[:, c * T:(c + 1) * T], hi[:, kt, cc_], lo[:, kt, cc_], xhi[:, kt, :],
                                   xlo[:, kt, :], kt == 0, kt == KT - 1)
                return mm

            def token_major(o, n):
                hi, lo = slab_views(n, KT)
                for tt in range(TT):
                    for kt in range(KT):
                        t_ = slice(tt * P, (tt + 1) * P)
                        mm = three(o[:, tt * 256:(tt + 1) * 256], xhi[:, kt, t_], xlo[:, kt, t_], hi[:, kt, :],
                                   lo[:, kt, :], kt == 0, kt == KT - 1)
                return mm

            def project(stage, name, how, norm=None):
                n = AT[(stage, name)]
                take_bank(pe, name)
                pe.wait_ge(lo_made, n + 1)
                ins = how(bank(name), n) if norm is None else how(bank(name), n, norm)
                ins.then_inc(*fills(name))

            def small_product(name, cols, norm=None):
                take_bank(pe, name)
                pe.wait_ge(s("small_lo"), 2)
                for kt in range(KT):
                    turned(norm, kt)
                    mm = three(bank(name)[:, 0:T], smh[:, kt, cols], sml[:, kt, cols], xhi[:, kt, :], xlo[:, kt, :],
                               kt == 0, kt == KT - 1)
                mm.then_inc(*fills(name))

            def out_slab(n, chunks, yh, yl, accs, first, last):
                hi, lo = slab_views(n, 2)
                for q in range(4):
                    tt, nh = q // 2, q % 2
                    for j in range(2):
                        mm = three(accs[q], yh[:, chunks[j], tt * P:(tt + 1) * P], yl[:, chunks[j], tt * P:(tt + 1) * P],
                                   hi[:, j, nh * 512:(nh + 1) * 512], lo[:, j, nh * 512:(nh + 1) * 512],
                                   first and j == 0, last and j == 1)
                    if last and q == 1:
                        mm.then_inc(s("first_tile_out"), 1)
                return mm

            pe.wait_ge(s("zeros_made"), 1)
            turn(0)
            small_product("gg", slice(0, 128), 0)
            take_bank(pe, "gq")
            keep_clock("gq", 6)
            project("in1", "gq", feature_major)
            take_bank(pe, "z")
            pe.wait_ge(s("vec_first_in"), 16)
            pe.wait_ge(*given_back("gg"))
            for c in range(2):
                mm = pe.matmul(bank("z")[:, c * T:(c + 1) * T], V("wup")[0:GATE_RANK, c * P:(c + 1) * P],
                               ggT[0:GATE_RANK, :], start=True, stop=True)
            mm.then_inc(*fills("z"))
            project("in1", "gk", feature_major)

            def level(L):
                if L:
                    i = GLA_LEVELS.index(L) - 1
                    pe.wait_ge(s("level_scaled"), i + 1)
                    q_, k_ = Dl[i % 2], Kl[i % 2]
                else:
                    pe.wait_ge(*given_back("gq"))
                    pe.wait_ge(*given_back("gk"))
                    q_, k_ = gqT, gkT
                for par in range(2):
                    take_bank(pe, f"lev{L}_{par}")
                    o, r = bank(f"lev{L}_{par}"), slice(64 * par, 64 * par + 64)
                    for c in range(2):
                        if L == 128:
                            mm = pe.matmul(o[:, c * P:(c + 1) * P], k_[r, c, 0:P], q_[r, c, P:T], start=True, stop=True)
                        else:
                            for blk in range(2):
                                b = slice(blk * P, (blk + 1) * P)
                                mm = pe.matmul(o[:, (2 * c + blk) * P:(2 * c + blk + 1) * P], k_[r, c, b], q_[r, c, b],
                                               start=True, stop=True)
                    mm.then_inc(*fills(f"lev{L}_{par}"))

            def rotate(name):
                take_bank(pe, name + "r")
                pe.wait_ge(*given_back(name))
                pe.matmul(bank(name + "r"), C(C_ROT), qpre[ROPED.index(name) % 2].rearrange("p a b -> p (a b)"), start=True, stop=True)\
                  .then_inc(*fills(name + "r"))

            pe.wait_ge(s("cst_rest_in"), 16)
            def softmax_scores(i, name):
                take_bank(pe, name)
                o = bank(name)
                r, c = slice(64 * (i % 2), 64 * (i % 2) + 64), i // 2
                pe.wait_ge(s("roped"), 2 if i < 4 else 4)
                pe.matmul(o[:, 0:P], qT[r, c, 0:P], kT[r, c, 0:P], start=True, stop=True)
                pe.matmul(o[:, P:3 * P], qT[r, c, P:T], kT[r, c, :], start=True, stop=True).then_inc(*fills(name))

            def turn_probs(hh, name, pex):
                take_bank(pe, name)
                pe.wait_ge(s("probs_made"), hh + 1)
                for j in range(3):
                    mm = pe.transpose(bank(name)[:, j * P:(j + 1) * P], pex[hh % 2][:, j * P:(j + 1) * P], ident)
                mm.then_inc(*fills(name))

            def values(i, hh, turned, name, pt, v0, v1, ready, signal=None):
                if i % 2 == 0:
                    take_bank(pe, name)
                pe.wait_ge(*ready)
                r = slice(64 * (i % 2), 64 * (i % 2) + 64)
                pe.matmul(bank(name)[r, 0:T], v0, pt[:, 0:T], start=True, stop=False)
                mm = pe.matmul(bank(name)[r, P:T], v1, pt[:, T:T + P], start=False, stop=True)
                return mm

            def moba_values(i):
                cols = slice((i % 4) * HD, (i % 4 + 1) * HD)
                mm = values(i, i, f"mt{i}", f"mo{i // 2}", pt1[i % 2], mv[:, 0, i // 4, cols], mv[:, 1, i // 4, cols],
                            given_back(f"mt{i}"))
                return mm

            def gla_values(hh):
                name, o = f"go{hh // 2}", hh % 2 * T
                if hh % 2 == 0:
                    take_bank(pe, name)
                cols = slice((hh % 2) * GLA_V, (hh % 2 + 1) * GLA_V)
                pe.matmul(bank(name)[:, o:o + T], gv[:, 0, hh // 2, cols],
                          Acat[:, hh, 0:2, :].rearrange("p a b -> p (a b)"), start=True, stop=False)
                mm = pe.matmul(bank(name)[:, o + P:o + T], gv[:, 1, hh // 2, cols], Acat[:, hh, 2, :], start=False,
                               stop=True)
                if hh % 2:
                    mm.then_inc(*fills(name))

            def gla_sums(j):
                take_bank(pe, f"gs{j}")
                pe.wait_ge(s("o_sq"), j + 1)
                pe.matmul(bank(f"gs{j}"), ones, osq[j].rearrange("p a b -> p (a b)"), start=True, stop=True)\
                  .then_inc(*fills(f"gs{j}"))

            for k in range(2, 12):
                name = IN1[k]
                project("in1", name, token_major if name[1] == "v" else feature_major)
                if k == 10:
                    pe.wait_ge(s("scores_added"), 2 * (len(MASKED_LEVELS) - 1))
                    pe.wait_ge(*given_back("lev128_1"))
                    pe.wait_ge(*given_back("gv1"))
                    for hh in range(GLA_H):
                        gla_values(hh)
                if k == 11:
                    for j in range(2):
                        gla_sums(j)
                if IN1[k - 1] in ROPED:
                    rotate(IN1[k - 1])
                if k >= 5:
                    softmax_scores(k - 5, f"ms{k - 5}")
                if k >= 6:
                    turn_probs(k - 6, f"mt{k - 6}", pex1)
                if k >= 7:
                    if k == 7:
                        pe.wait_ge(*given_back("mv0"))
                    if k == 11:
                        pe.wait_ge(*given_back("mv1"))
                    moba_values(k - 7).then_inc(*pv_signal(k - 7))
                for L in levels_after.get(k, []):
                    level(L)

            def out_1(c):
                n = OUT1[c]
                k, s_ = int(n[1:]), AT[("out1", n)]
                if c == 0:
                    for q in range(4):
                        take_bank(pe, f"w1_{q}")
                if k < 2:
                    pe.wait_ge(*given_back(f"mo{2 * k + 1}"))
                else:
                    pe.wait_ge(s("gy_lo"), k - 1)
                pe.wait_ge(lo_made, s_ + 1)
                out_slab(s_, (2 * k, 2 * k + 1), yhi, ylo, [bank(f"w1_{q}") for q in range(4)], c == 0,
                         c == len(OUT1) - 1)\
                    .then_inc(proj_used["out1"], 1)

            out_1(0)
            softmax_scores(7, "ms7")
            turn_probs(6, "mt6", pex1)
            moba_values(5).then_inc(*pv_signal(5))
            out_1(1)
            turn_probs(7, "mt7", pex1)
            moba_values(6).then_inc(*pv_signal(6))
            moba_values(7).then_inc(*pv_signal(7))
            out_1(2)
            out_1(3)
            turn(1)

            def ffn_up(k, f, i=None):
                norm = {"ffn1": 1, "ffn2": 3}[k]
                n = AT[(k, f"g{f}")]
                for j in range(2):
                    if i is not None or f >= 2 or ffn_lease[k][2 * (f % 2) + j][1]:
                        pe.wait_ge(*hidden_free(k, f, j, i, done=False))
                    pe.wait_ge(lo_made, n + j + 1 if i is None else n + j + 1 + 6 * i)
                    feature_major(hidden(k, f, j), n + j, norm if (f, j) == (0, 0) else None).then_inc(hidden_full(k, f, j)[0], 1)

            def ffn_down(k, f, i=None):
                n = AT[(k, f"d{f}")]
                if f == 0:
                    for q in range(4):
                        take_bank(pe, f"{k}_acc{q}")
                pe.wait_ge(s(f"g_lo_{k}"), f + 1 if i is None else f + 1 + 2 * i)
                pe.wait_ge(lo_made, n + 1 if i is None else n + 1 + 6 * i)
                par = f % 2
                out_slab(n, (2 * par, 2 * par + 1), yhi, ylo, [bank(f"{k}_acc{q}") for q in range(4)], f == 0,
                         f == FF - 1)\
                    .then_inc(down_used[k], 1)

            def ffn(k):
                ffn_up(k, 0)
                ffn_up(k, 1)
                ffn_down(k, 0)
                with pe.Fori(0, FFN_PAIRS) as i:
                    for f in (2, 3):
                        ffn_up(k, f, i)
                        ffn_down(k, f - 1, i)
                ffn_up(k, FF - 3)
                ffn_down(k, FF - 4)
                ffn_up(k, FF - 2)
                ffn_up(k, FF - 1)
                for f in range(FF - 3, FF):
                    ffn_down(k, f)

            ffn("ffn1")
            turn(2)
            def stick_scores(i):
                name = f"ss{i}"
                take_bank(pe, name)
                pe.wait_ge(*given_back("sk"))
                o, r, c = bank(name), slice(64 * (i % 2), 64 * (i % 2) + 64), i // 2
                pe.matmul(o[:, 0:T], skT[r, c, 0:P], sqT[r, c, :], start=True, stop=True)
                pe.matmul(o[:, T:T + P], skT[r, c, P:T], sqT[r, c, P:T], start=True, stop=True).then_inc(*fills(name))

            def stick_sums(i):
                name = f"sr{i}"
                take_bank(pe, name)
                pe.wait_ge(s("stick_soft"), i + 1)
                pe.matmul(bank(name)[:, 0:3 * P], C(C_SUF), Lt[i % 2], start=True, stop=False)
                pe.matmul(bank(name)[:, P:2 * P], ones, Lt[i % 2][:, 2 * P:3 * P], start=False, stop=True)\
                  .then_inc(*fills(name))

            def stick_values(i):
                cols = slice(i * HD, (i + 1) * HD)
                mm = values(i, i, None, f"so{i // 2}", wt[i % 2], sv[:, 0, cols], sv[:, 1, cols], (s("stick_w"), i + 1))
                return mm

            def fox_scores(i):
                name = f"fs{i}"
                take_bank(pe, name)
                pe.wait_ge(*given_back("fk"))
                pe.wait_ge(s("forget_made"), 1)
                o = bank(name)
                pe.matmul(o[:, 0:P], fqp[:, i, 0:P], fkp[:, i, 0:P], start=True, stop=True)
                mm = pe.matmul(o[:, P:3 * P], fqp[:, i, P:T], fkp[:, i, :], start=True, stop=True)
                mm.then_inc(*fills(name))

            def fox_values(i):
                cols = slice(i * HD, (i + 1) * HD)
                return values(i, 8 + i, None, f"fo{i // 2}", pt2[i % 2], fv[:, 0, cols], fv[:, 1, cols],
                              given_back(f"ft{i}"))

            def fox_norm(j):
                name = ("fqs", "fks")[j]
                take_bank(pe, name)
                pe.wait_ge(s("f_sq"), j + 1)
                pe.matmul(bank(name), C(C_HEAD), fsq[j].rearrange("p a b -> p (a b)"), start=True, stop=True)\
                  .then_inc(*fills(name))

            def spatial_gate():
                take_bank(pe, "gm")
                pe.wait_ge(s("v_normed"), 1)
                wsp = V("wsp").rearrange("p (a b) -> p a b", a=4)
                for g in range(4):
                    r = slice(64 * (g % 2), 64 * (g % 2) + 64)
                    for c in range(2):
                        at = (g // 2) * T + c * P
                        mm = pe.matmul(bank("gm")[r, at:at + P], vn[:, c, g * 64:(g + 1) * 64], wsp[:, g, :],
                                       start=True, stop=True)
                mm.then_inc(*fills("gm"))

            for k, name in enumerate(IN2 + EARLY):
                how = token_major if name in ("sv", "fv", "v") else feature_major
                project("in2", name, how, 2 if k == 0 else None)
                if k == 6:
                    for j in range(2):
                        fox_norm(j)
                if 2 <= k <= 5:
                    stick_scores(k - 2)
                if 3 <= k <= 6:
                    stick_sums(k - 3)
                if 4 <= k <= 7:
                    pe.wait_ge(*given_back("sv"))
                    stick_values(k - 4).then_inc(*stick_signal(k - 4))
                if k == 7:
                    small_product("f", slice(16, 144))
                if 9 <= k <= 12:
                    fox_scores(k - 9)
                if 10 <= k <= 13:
                    turn_probs(8 + k - 10, f"ft{k - 10}", pex2)
                if 11 <= k <= 14:
                    pe.wait_ge(*given_back("fv"))
                    fox_values(k - 11).then_inc(*pv_signal(8 + k - 11))
                if k == 17:
                    spatial_gate()

            def mix_out(m):
                n = AT[("mix2", f"o{m}")]
                if m == 0:
                    for q in range(4):
                        take_bank(pe, f"w2_{q}")
                pe.wait_ge(s("merged_lo"), m + 1)
                pe.wait_ge(lo_made, n + 1)
                out_slab(n, (2 * (m % 2), 2 * (m % 2) + 1), mh_all, ml_all, [bank(f"w2_{q}") for q in range(4)],
                         m == 0, m == 3)\
                    .then_inc(proj_used["mix2"], 1)

            for m in range(4):
                for j in range(2):
                    project("mix2", f"l{2 + j}_{m}", feature_major)
                n_ = AT[("mix2", f"m{m}")]
                pe.wait_ge(lo_made, n_ + 1)
                if m == 0:
                    pe.wait_ge(s("y_lo"), 2)
                    pe.wait_ge(*given_back("so1"))
                    pe.wait_ge(*given_back("fo1"))
                hi, lo = [t[:, n_ % SPLIT, :].rearrange("p (n k c) -> p n k c", n=4, k=2) for t in (hiw, low)]
                for n in range(N_BRANCH):
                    take_bank(pe, f"br{m}_{n}")
                    for c in range(2):
                        for k in range(2):
                            c_ = slice(c * P, (c + 1) * P)
                            mm = three(bank(f"br{m}_{n}")[:, c * T:(c + 1) * T], hi[:, n, k, c_], lo[:, n, k, c_],
                                       yhi[:, 2 * n + k, :], ylo[:, 2 * n + k, :], k == 0, k == 1)
                    mm.then_inc(*fills(f"br{m}_{n}"))
                if m:
                    mix_out(m - 1)
            mix_out(3)
            turn(3)
            ffn("ffn2")


_INS = ["x", "slabs", "vec", "cst"]


def constants():
    c = np.zeros((P, C_W), np.float32)
    i, j = np.arange(P)[:, None], np.arange(P)[None, :]
    c[:, C_ID:C_ID + P] = i == j
    c[:, C_NEG:C_NEG + P] = np.where(j > i, NEG, 0)
    half = HD // 2
    for k in range(P):
        if k % HD < half:
            c[k + half, C_ROT + k] = -1
        else:
            c[k - half, C_ROT + k] = 1
    freq = (1.0 / (np.float32(10000.0) ** (np.arange(0, HD, 2, dtype=np.float32) / np.float32(HD)))).astype(np.float32)
    ang = (np.arange(T, dtype=np.float32)[None, :] * freq[np.arange(P) % half][:, None]).astype(np.float32)
    c[:, C_COS:C_COS + T] = np.cos(ang)
    c[:, C_SIN:C_SIN + T] = np.sin(ang)
    for n, L in enumerate(MASKED_LEVELS):
        m = (i == j) if L == 0 else (i // (2 * L) == j // (2 * L)) & (i % (2 * L) < L) & (j % (2 * L) >= L)
        c[:, C_LEV + n * P:C_LEV + (n + 1) * P] = m
    c[:, C_HEAD:C_HEAD + P] = i // HD == j // HD
    c[:, C_ONE:C_ONE + P] = 1
    c[:, C_SUF:C_SUF + P] = i >= j
    c[:, C_STN:C_STN + P] = np.where(i >= j, NEG, 0)
    c[:, C_TRI:C_TRI + P] = i <= j
    for k in range(FOX_H):
        other = HD * (1 - k % 2)
        c[other + 32 + k // 2, C_SEL + k] = 1
        c[other + k // 2, C_SEL + 4 + k] = 1
    c[:, C_EPS] = EPS
    c[:, C_MHALF:C_MHALF + 2] = -0.5
    return c


def columns(w, at, n=SLAB_W):
    return w[:, at:at + n].reshape(KT, P, n).transpose(1, 0, 2)


def rows(w, at):
    return w[256 * at:256 * (at + 1)].reshape(2, P, D).transpose(1, 0, 2)


IN1_AT = {"mq0": 0, "mq1": 256, "mk0": 512, "mk1": 768, "mv0": 1024, "mv1": 1280, "gq": 1536, "gk": 1792, "gv0": 2048,
          "gv1": 2304, "gr0": 2560, "gr1": 2816}
IN2_AT = {"cb": 0, "cc": 256, "cx": 512, "u": 768, "v": 1024, "sq": 1280, "sk": 1536, "sv": 1792, "fq": 2048,
          "fk": 2304, "fv": 2560}
GATE_AT = 2820


def slab(stage, name, w):
    k = int(name[1:]) if name[1:].isdigit() else 0
    if stage == "in1":
        return columns(w["w_in"], IN1_AT[name])
    if stage == "in2":
        if name[0] == "e":
            return columns(w["w_in_2"], GATE_AT + D * int(name[1]) + 256 * int(name[3]))
        return columns(w["w_in_2"], IN2_AT[name])
    if stage == "out1":
        return rows(w["w_out"], k)
    if stage == "mix2":
        if name[0] == "l":
            return columns(w["w_in_2"], GATE_AT + D * int(name[1]) + 256 * int(name[3]))
        if name[0] == "o":
            return rows(w["w_out_2"], k)
        return w["w_branch_2"][:, :, 256 * k:256 * (k + 1)].reshape(4, 2, P, 256).transpose(2, 0, 1, 3)
    up, down = ("w_ffn_up", "w_ffn_down") if stage == "ffn1" else ("w_ffn_in_2", "w_ffn_out_2")
    if name[0] == "d":
        return rows(w[down], k)
    return columns(w[up], 256 * k + (D_FF if name[0] == "v" else 0))


def chunked(v):
    return v.reshape(-1, P).T


def small_inputs(w):
    v = np.zeros((P, V_W), np.float32)

    def put(name, a):
        lo, hi = V_LAY[name]
        v[0:a.shape[0], lo:hi] = a

    for n, name in enumerate(("attn_norm_g", "ffn_norm_g", "norm_mix_g_2", "norm_ffn_g_2")):
        put(f"ng{n}", chunked(w[name]))
    put("bgate", chunked(w["b_gate"]))
    put("glag", w["gla_norm_g"].T)
    put("cw", chunked(w["conv_w"]))
    put("cb", chunked(w["conv_b"]))
    put("wc2", chunked(w["w_conv_2"]))
    put("fqg", np.concatenate([w["fox_q_norm_g_2"]] * 2)[:, None])
    put("fkg", np.concatenate([w["fox_k_norm_g_2"]] * 2)[:, None])
    f_rows = np.array([1, 3, 1, 3, 0, 2, 0, 2])
    bf = np.zeros((4, 32), np.float32)
    bf[:, 0:2] = w["fox_forget_b_2"][f_rows].reshape(4, 2)
    put("bf", bf.reshape(P, 1))
    put("wup", w["w_gate_up"])
    small = np.concatenate([w["w_in"][:, 3072:3088], w["w_in_2"][:, 2816:2820][:, f_rows]], axis=1)
    put("small", small.reshape(KT, P, 24).transpose(1, 0, 2).reshape(P, KT * 24))
    put("fg", np.broadcast_to(w["final_norm_g"], (P, D)))
    put("lng", np.broadcast_to(w["gmlp_ln_g_2"], (P, 256)))
    put("lnb", np.broadcast_to(w["gmlp_ln_b_2"], (P, 256)))
    put("bsp", np.repeat(w["b_spatial_2"].reshape(2, 2, 1, P), 64, axis=2).reshape(2, P, P).transpose(1, 0, 2)
        .reshape(P, 256))
    put("wsp", w["w_spatial_2"].transpose(2, 0, 1).reshape(P, 512))
    return v


def kernel(**inputs):
    import concourse.bacc as _bacc
    from concourse.bass_utils import run_bass_kernel_spmd as _run

    w = {}
    for name, a in inputs.items():
        a = np.asarray(a)
        w[name] = a if name == "final_norm_g" or name == "x" else a[0]
    arrays = {
        "in_x": np.ascontiguousarray(w["x"][0]),
        "in_slabs": np.stack([slab(stage, name, w).reshape(P, SLAB) for stage, name in STREAM]),
        "in_vec": small_inputs(w),
        "in_cst": constants(),
    }
    nc = _bacc.Bacc("TRN2", target_bir_lowering=False, num_devices=1)
    args = [nc.dram_tensor(n, a.shape, F32, kind="ExternalInput").ap() for n, a in arrays.items()]
    args.append(nc.dram_tensor("out_0", (T, D), F32, kind="ExternalOutput").ap())
    build(nc, *args)
    r = _run(nc, [arrays], core_ids=[0])
    return r.results[0]["out_0"].reshape(1, T, D)
```
